# Optimizing a Trainium2 kernel written in Bass

```python
import jax, jax.numpy as jnp
from jax import lax
import numpy as np
import math

D_MODEL = 1024
BATCH = 1
SEQ = 512
DEPTH = 2

N_A = DEPTH // 2
N_B = DEPTH - N_A
N_META = 16
POOL_WINDOWS = (2, 4, 8, 16)
N_POOL_GROUPS = len(POOL_WINDOWS)
POOL_GROUP_DIM = D_MODEL // N_POOL_GROUPS
MAX_WINDOW = max(POOL_WINDOWS)
N_HEADS = 8
QK_NOPE_DIM = 128
QK_ROPE_DIM = 64
V_HEAD_DIM = 128
Q_LORA_RANK = 384
KV_LORA_RANK = 256
ROPE_THETA = 10000.0
ATTN_SCALE = (QK_NOPE_DIM + QK_ROPE_DIM) ** -0.5
Q_BLOCK = 128
N_EXPERT_GROUPS = 4
EXPERTS_PER_GROUP = 8
N_EXPERTS = N_EXPERT_GROUPS * EXPERTS_PER_GROUP
TOP_K_IN_GROUP = 2
D_EXPERT = 256
MOE_GROUP_ROWS = 256
RMS_EPS = 1e-6
NEG_INF = -1e30


def rmsnorm(x, g):
    xf = x.astype(jnp.float32)
    y = xf * lax.rsqrt(jnp.mean(xf * xf, axis=-1, keepdims=True) + RMS_EPS)
    return (y * g.astype(jnp.float32)).astype(x.dtype)

def rope_tables(length):
    pos = jnp.arange(length, dtype=jnp.float32)
    inv_freq = ROPE_THETA ** (-jnp.arange(0, QK_ROPE_DIM, 2, dtype=jnp.float32) / QK_ROPE_DIM)
    ang = pos[:, None] * inv_freq[None, :]
    return jnp.cos(ang), jnp.sin(ang)

def apply_rope(x, cos, sin):
    xf = x.astype(jnp.float32)
    half = xf.shape[-1] // 2
    x1, x2 = xf[..., :half], xf[..., half:]
    return jnp.concatenate([x1 * cos - x2 * sin, x1 * sin + x2 * cos], axis=-1).astype(x.dtype)

def pool_mixer(h, w_grp, scale):
    L_ = h.shape[1]
    hf = h.astype(jnp.float32)
    cs = jnp.pad(jnp.cumsum(hf, axis=1), ((0, 0), (MAX_WINDOW, 0), (0, 0)))
    t = jnp.arange(L_)
    outs = []
    for g, w in enumerate(POOL_WINDOWS):
        sl = slice(g * POOL_GROUP_DIM, (g + 1) * POOL_GROUP_DIM)
        win_sum = cs[:, MAX_WINDOW:, sl] - cs[:, MAX_WINDOW - w:MAX_WINDOW - w + L_, sl]
        cnt = jnp.minimum(t + 1, w).astype(jnp.float32)[None, :, None]
        pooled = (win_sum / cnt - hf[:, :, sl]).astype(h.dtype)
        outs.append(jnp.einsum('blc,cd->bld', pooled, w_grp[g]))
    return jnp.concatenate(outs, axis=-1) * scale

def shared_latent_kv(h, kv_norm, w_dkv, kv_lat_norm, w_uk, w_uv, cos, sin):
    c = jnp.einsum('bld,dr->blr', rmsnorm(h, kv_norm), w_dkv)
    c_kv = rmsnorm(c[..., :KV_LORA_RANK], kv_lat_norm)
    k_rope = apply_rope(c[..., KV_LORA_RANK:], cos, sin)
    k_nope = jnp.einsum('blr,rhd->blhd', c_kv, w_uk)
    v = jnp.einsum('blr,rhd->blhd', c_kv, w_uv)
    return k_nope, k_rope, v

def causal_block_attention(q_nope, q_rope, k_nope, k_rope, v):
    B_, L_, H_, _ = q_nope.shape
    nb = -(-L_ // Q_BLOCK)
    Lp = nb * Q_BLOCK
    pad = Lp - L_
    padf = lambda a: jnp.pad(a, [(0, 0), (0, pad)] + [(0, 0)] * (a.ndim - 2))
    qn, qr, kn, kr, vv = padf(q_nope), padf(q_rope), padf(k_nope), padf(k_rope), padf(v)
    to_blocks = lambda a: jnp.moveaxis(a.reshape((B_, nb, Q_BLOCK) + a.shape[2:]), 1, 0)
    kpos = jnp.arange(Lp)

    def one_block(args):
        qn_b, qr_b, b_idx = args
        s = (jnp.einsum('bqhd,bkhd->bhqk', qn_b, kn, preferred_element_type=jnp.float32)
             + jnp.einsum('bqhr,bkr->bhqk', qr_b, kr, preferred_element_type=jnp.float32)) * ATTN_SCALE
        qpos = b_idx * Q_BLOCK + jnp.arange(Q_BLOCK)
        s = jnp.where(kpos[None, :] <= qpos[:, None], s, NEG_INF)
        p = jax.nn.softmax(s, axis=-1)
        return jnp.einsum('bhqk,bkhd->bqhd', p.astype(vv.dtype), vv)

    o = lax.map(one_block, (to_blocks(qn), to_blocks(qr), jnp.arange(nb)))
    return jnp.moveaxis(o, 0, 1).reshape(B_, Lp, H_, V_HEAD_DIM)[:, :L_]

def mla_mixer(hn, w_dq, q_norm, w_uq, w_o, k_nope, k_rope, v, cos, sin):
    B_, L_, _ = hn.shape
    cq = rmsnorm(jnp.einsum('bld,dr->blr', hn, w_dq), q_norm)
    q = jnp.einsum('blr,rhd->blhd', cq, w_uq)
    q_nope = q[..., :QK_NOPE_DIM]
    q_rope = apply_rope(q[..., QK_NOPE_DIM:], cos[:, None, :], sin[:, None, :])
    o = causal_block_attention(q_nope, q_rope, k_nope, k_rope, v)
    return jnp.einsum('blf,fd->bld', o.reshape(B_, L_, N_HEADS * V_HEAD_DIM), w_o)

def hierarchical_moe(h, wr_g, br_g, wr_e, br_e, w_gate, w_up, w_down):
    B_, L_, D_ = h.shape
    xt = h.reshape(-1, D_)
    n_tok = xt.shape[0]
    xf = xt.astype(jnp.float32)
    p_g = jax.nn.softmax(xf @ wr_g.astype(jnp.float32) + br_g.astype(jnp.float32), axis=-1)
    g_sel = jnp.argmax(p_g, axis=-1)
    w_g = jnp.max(p_g, axis=-1)
    logit_e = (xf @ wr_e.astype(jnp.float32) + br_e.astype(jnp.float32)).reshape(n_tok, N_EXPERT_GROUPS, EXPERTS_PER_GROUP)
    sel = jnp.take_along_axis(logit_e, g_sel[:, None, None], axis=1)[:, 0]
    top_v, top_i = lax.top_k(sel, TOP_K_IN_GROUP)
    gate = w_g[:, None] * jax.nn.softmax(top_v, axis=-1)
    eid = (g_sel[:, None] * EXPERTS_PER_GROUP + top_i).reshape(-1).astype(jnp.int32)
    tid = jnp.repeat(jnp.arange(n_tok, dtype=jnp.int32), TOP_K_IN_GROUP)
    wt = gate.reshape(-1)
    n_assign = n_tok * TOP_K_IN_GROUP
    order = jnp.argsort(eid)
    e_sorted = eid[order]
    counts = jnp.bincount(eid, length=N_EXPERTS)
    starts = jnp.cumsum(counts) - counts
    padded = (counts + MOE_GROUP_ROWS - 1) // MOE_GROUP_ROWS * MOE_GROUP_ROWS
    pends = jnp.cumsum(padded)
    pstarts = pends - padded
    dest = pstarts[e_sorted] + (jnp.arange(n_assign) - starts[e_sorted])
    n_blocks = -(-(n_assign + N_EXPERTS * (MOE_GROUP_ROWS - 1)) // MOE_GROUP_ROWS)
    n_rows = n_blocks * MOE_GROUP_ROWS
    row_tok = jnp.full((n_rows,), n_tok, jnp.int32).at[dest].set(tid[order])
    row_w = jnp.zeros((n_rows,), h.dtype).at[dest].set(wt[order].astype(h.dtype))
    block_e = jnp.minimum(jnp.searchsorted(pends, jnp.arange(n_blocks) * MOE_GROUP_ROWS, side='right'), N_EXPERTS - 1)
    x_rows = jnp.concatenate([xt, jnp.zeros((1, D_), xt.dtype)], axis=0)[row_tok]
    x_rows = x_rows.reshape(n_blocks, MOE_GROUP_ROWS, D_)

    def expert_block(args):
        e, xb = args
        return (jax.nn.silu(xb @ w_gate[e]) * (xb @ w_up[e])) @ w_down[e]

    y = lax.map(expert_block, (block_e, x_rows)).reshape(n_rows, D_)
    out = jnp.zeros((n_tok + 1, D_), h.dtype).at[row_tok].add(y * row_w[:, None])[:n_tok]
    return out.reshape(B_, L_, D_)

def first_inputs(seed: int = 0) -> dict:
    key = jax.random.key(seed)
    ks = jax.random.split(key, 32)
    f32 = jnp.float32
    nrm = lambda k, shape, fan: jax.random.normal(k, shape, f32) * (fan ** -0.5)
    gain = lambda k, shape: 1.0 + 0.05 * jax.random.normal(k, shape, f32)
    return {
        "x": jax.random.normal(ks[0], (BATCH, SEQ, D_MODEL), f32),
        "meta_tokens": jax.random.normal(ks[1], (N_META, D_MODEL), f32),
        "a_norm": gain(ks[2], (N_A, D_MODEL)),
        "a_w": nrm(ks[3], (N_A, N_POOL_GROUPS, POOL_GROUP_DIM, POOL_GROUP_DIM), POOL_GROUP_DIM),
        "a_scale": gain(ks[4], (N_A, D_MODEL)),
        "b_norm": gain(ks[5], (N_B, D_MODEL)),
        "b_w_dq": nrm(ks[6], (N_B, D_MODEL, Q_LORA_RANK), D_MODEL),
        "b_q_norm": gain(ks[7], (N_B, Q_LORA_RANK)),
        "b_w_uq": nrm(ks[8], (N_B, Q_LORA_RANK, N_HEADS, QK_NOPE_DIM + QK_ROPE_DIM), Q_LORA_RANK),
        "b_w_o": nrm(ks[9], (N_B, N_HEADS * V_HEAD_DIM, D_MODEL), N_HEADS * V_HEAD_DIM),
        "kv_norm": gain(ks[10], (D_MODEL,)),
        "w_dkv": nrm(ks[11], (D_MODEL, KV_LORA_RANK + QK_ROPE_DIM), D_MODEL),
        "kv_lat_norm": gain(ks[12], (KV_LORA_RANK,)),
        "w_uk": nrm(ks[13], (KV_LORA_RANK, N_HEADS, QK_NOPE_DIM), KV_LORA_RANK),
        "w_uv": nrm(ks[14], (KV_LORA_RANK, N_HEADS, V_HEAD_DIM), KV_LORA_RANK),
        "ffn_norm": gain(ks[15], (DEPTH, D_MODEL)),
        "router_g": nrm(ks[16], (DEPTH, D_MODEL, N_EXPERT_GROUPS), D_MODEL),
        "router_g_bias": 0.01 * jax.random.normal(ks[17], (DEPTH, N_EXPERT_GROUPS), f32),
        "router_e": nrm(ks[18], (DEPTH, D_MODEL, N_EXPERTS), D_MODEL),
        "router_e_bias": 0.01 * jax.random.normal(ks[19], (DEPTH, N_EXPERTS), f32),
        "w_gate": nrm(ks[20], (DEPTH, N_EXPERTS, D_MODEL, D_EXPERT), D_MODEL),
        "w_up": nrm(ks[21], (DEPTH, N_EXPERTS, D_MODEL, D_EXPERT), D_MODEL),
        "w_down": nrm(ks[22], (DEPTH, N_EXPERTS, D_EXPERT, D_MODEL), D_EXPERT),
        "final_norm": gain(ks[23], (D_MODEL,)),
    }

def first_block(x, meta_tokens, a_norm, a_w, a_scale, b_norm, b_w_dq, b_q_norm, b_w_uq, b_w_o,
              kv_norm, w_dkv, kv_lat_norm, w_uk, w_uv, ffn_norm, router_g, router_g_bias,
              router_e, router_e_bias, w_gate, w_up, w_down, final_norm):
    B_, S_, D_ = x.shape
    h = jnp.concatenate([jnp.broadcast_to(meta_tokens[None].astype(x.dtype), (B_, N_META, D_)), x], axis=1)
    L_ = S_ + N_META
    cos, sin = rope_tables(L_)
    k_nope = k_rope = v = None
    for layer in range(DEPTH):
        if layer < N_A:
            i = layer
            h = h + pool_mixer(rmsnorm(h, a_norm[i]), a_w[i], a_scale[i])
        else:
            i = layer - N_A
            h = h + mla_mixer(rmsnorm(h, b_norm[i]), b_w_dq[i], b_q_norm[i], b_w_uq[i], b_w_o[i],
                              k_nope, k_rope, v, cos, sin)
        h = h + hierarchical_moe(rmsnorm(h, ffn_norm[layer]), router_g[layer], router_g_bias[layer],
                                 router_e[layer], router_e_bias[layer], w_gate[layer], w_up[layer], w_down[layer])
        if layer == N_A - 1:
            k_nope, k_rope, v = shared_latent_kv(h, kv_norm, w_dkv, kv_lat_norm, w_uk, w_uv, cos, sin)
    return rmsnorm(h, final_norm)[:, N_META:]


RG_WIDTH = D_MODEL // 2
RG_BLOCKS = 8
RG_BLOCK = RG_WIDTH // RG_BLOCKS
CONV_WIDTH = 4
RG_C = 8.0
GLA_HEADS = 4
GLA_VDIM = D_MODEL // 2
GLA_KDIM = GLA_VDIM // 2
GLA_HK = GLA_KDIM // GLA_HEADS
GLA_HV = GLA_VDIM // GLA_HEADS
GLA_LOWRANK = 16
GLA_GATE_TAU = 16.0
GLA_CHUNK = 64
EVEN_IN = 2 * RG_WIDTH + 2 * GLA_KDIM + 2 * GLA_VDIM + GLA_LOWRANK
MIX_WIDTH = RG_WIDTH + GLA_VDIM

FOX_HEADS = 16
FOX_HD = D_MODEL // FOX_HEADS
FOX_BLOCK = 128
ODD_IN = 4 * D_MODEL + FOX_HEADS

D_FF = 4 * D_MODEL
N_EVEN = (DEPTH + 1) // 2
N_ODD = DEPTH // 2
ALPHA = (2 * DEPTH) ** 0.25
BETA = (8 * DEPTH) ** -0.25
LN_EPS = 1e-5


def layer_norm(x, g, b):
    xf = x.astype(jnp.float32)
    mu = jnp.mean(xf, axis=-1, keepdims=True)
    var = jnp.mean(jnp.square(xf - mu), axis=-1, keepdims=True)
    return ((xf - mu) * lax.rsqrt(var + LN_EPS) * g.astype(jnp.float32)
            + b.astype(jnp.float32)).astype(x.dtype)

def rms_norm(x, g):
    xf = x.astype(jnp.float32)
    y = xf * lax.rsqrt(jnp.mean(xf * xf, axis=-1, keepdims=True) + RMS_EPS)
    return (y * g.astype(jnp.float32)).astype(x.dtype)

def ada_mod(c, w, b):
    m = (jax.nn.silu(c) @ w + b)[:, None, :]
    shift, scale, gate = jnp.split(m, 3, axis=-1)
    return shift, scale, 1.0 + gate

def causal_dwconv(x, w, b):
    k_len, ch = w.shape
    y = lax.conv_general_dilated(
        x, w[:, None, :].astype(x.dtype), window_strides=(1,),
        padding=[(k_len - 1, 0)], dimension_numbers=('NWC', 'WIO', 'NWC'),
        feature_group_count=ch)
    return y + b

def rg_lru(x, w_a, b_a, w_x, b_x, lam):
    bn, sn, _ = x.shape
    xf = x.astype(jnp.float32)
    xb = xf.reshape(bn, sn, RG_BLOCKS, RG_BLOCK)
    r = jax.nn.sigmoid(jnp.einsum('bsni,nij->bsnj', xb, w_a.astype(jnp.float32)).reshape(bn, sn, RG_WIDTH) + b_a)
    i = jax.nn.sigmoid(jnp.einsum('bsni,nij->bsnj', xb, w_x.astype(jnp.float32)).reshape(bn, sn, RG_WIDTH) + b_x)
    log_a = RG_C * r * jax.nn.log_sigmoid(lam.astype(jnp.float32))
    a = jnp.exp(log_a)
    u = jnp.sqrt(-jnp.expm1(2.0 * log_a)) * (i * xf)

    def combine(left, right):
        a1, h1 = left
        a2, h2 = right
        return a1 * a2, a2 * h1 + h2

    _, h = lax.associative_scan(combine, (a, u), axis=1)
    return h.astype(x.dtype)

def gla_chunked(q, k, v, log_alpha):
    bn, sn, nh, dk = q.shape
    dv = v.shape[-1]
    n_chunks = sn // GLA_CHUNK

    def blocks(t):
        return t.astype(jnp.float32).reshape(bn, n_chunks, GLA_CHUNK, nh, t.shape[-1]).transpose(1, 0, 3, 2, 4)

    qc = blocks(q) * (dk ** -0.5)
    kc = blocks(k)
    vc = blocks(v)
    bcum = jnp.cumsum(blocks(log_alpha), axis=3)
    b_last = bcum[:, :, :, -1:, :]
    q_dec = qc * jnp.exp(bcum)
    k_dec = kc * jnp.exp(-bcum)
    k_end = kc * jnp.exp(b_last - bcum)
    causal = jnp.tril(jnp.ones((GLA_CHUNK, GLA_CHUNK), dtype=bool))
    att = jnp.where(causal, jnp.einsum('nbhtd,nbhsd->nbhts', q_dec, k_dec), 0.0)
    o_intra = jnp.einsum('nbhts,nbhsv->nbhtv', att, vc)
    kv = jnp.einsum('nbhsd,nbhsv->nbhdv', k_end, vc)
    decay = jnp.exp(b_last[:, :, :, 0, :])

    def step(state, inp):
        dcy, kv_n = inp
        return dcy[..., None] * state + kv_n, state

    _, s_prev = lax.scan(step, jnp.zeros((bn, nh, dk, dv), jnp.float32), (decay, kv))
    o = o_intra + jnp.einsum('nbhtd,nbhdv->nbhtv', q_dec, s_prev)
    return o.transpose(1, 0, 3, 2, 4).reshape(bn, sn, nh, dv).astype(q.dtype)

def even_mixer(u, w_in, conv_w, conv_b, rg_wa, rg_ba, rg_wx, rg_bx, rg_lam,
               gla_w_up, gla_b_up, gla_norm_g, w_out):
    bn, sn, _ = u.shape
    proj = u @ w_in
    s1 = RG_WIDTH
    s2 = s1 + RG_WIDTH
    s3 = s2 + GLA_KDIM
    s4 = s3 + GLA_KDIM
    s5 = s4 + GLA_VDIM
    s6 = s5 + GLA_VDIM
    xr, yr, q, k, v, g, zl = jnp.split(proj, [s1, s2, s3, s4, s5, s6], axis=-1)
    h = rg_lru(causal_dwconv(xr, conv_w, conv_b), rg_wa, rg_ba, rg_wx, rg_bx, rg_lam)
    rg_out = h * jax.nn.gelu(yr)
    log_alpha = jax.nn.log_sigmoid((zl @ gla_w_up + gla_b_up).astype(jnp.float32)) / GLA_GATE_TAU
    o = gla_chunked(q.reshape(bn, sn, GLA_HEADS, GLA_HK),
                    k.reshape(bn, sn, GLA_HEADS, GLA_HK),
                    v.reshape(bn, sn, GLA_HEADS, GLA_HV),
                    log_alpha.reshape(bn, sn, GLA_HEADS, GLA_HK))
    o = rms_norm(o, gla_norm_g.reshape(GLA_HEADS, GLA_HV)) * jax.nn.silu(g).reshape(bn, sn, GLA_HEADS, GLA_HV)
    mix = jnp.concatenate([rg_out, o.reshape(bn, sn, GLA_VDIM)], axis=-1)
    return mix @ w_out

def fox_attention(u, w_in, b_f, q_norm_g, k_norm_g, w_out):
    bn, sn, _ = u.shape
    proj = u @ w_in
    q, k, v, g, fl = jnp.split(proj, [D_MODEL, 2 * D_MODEL, 3 * D_MODEL, 4 * D_MODEL], axis=-1)
    q = rms_norm(q.reshape(bn, sn, FOX_HEADS, FOX_HD), q_norm_g).transpose(0, 2, 1, 3) * (FOX_HD ** -0.5)
    k = rms_norm(k.reshape(bn, sn, FOX_HEADS, FOX_HD), k_norm_g).transpose(0, 2, 1, 3)
    v = v.reshape(bn, sn, FOX_HEADS, FOX_HD).transpose(0, 2, 1, 3)
    log_f = jax.nn.log_sigmoid((fl + b_f).astype(jnp.float32))
    f_cum = jnp.cumsum(log_f, axis=1).transpose(0, 2, 1)
    outs = []
    for blk in range(sn // FOX_BLOCK):
        t0 = blk * FOX_BLOCK
        t1 = t0 + FOX_BLOCK
        s = jnp.einsum('bhtd,bhsd->bhts', q[:, :, t0:t1], k[:, :, :t1]).astype(jnp.float32)
        s = s + f_cum[:, :, t0:t1, None] - f_cum[:, :, None, :t1]
        mask = (t0 + jnp.arange(FOX_BLOCK))[:, None] >= jnp.arange(t1)[None, :]
        p = jax.nn.softmax(jnp.where(mask, s, -jnp.inf), axis=-1)
        outs.append(jnp.einsum('bhts,bhsd->bhtd', p.astype(v.dtype), v[:, :, :t1]))
    o = jnp.concatenate(outs, axis=2).transpose(0, 2, 1, 3).reshape(bn, sn, D_MODEL)
    return (o * jax.nn.sigmoid(g)) @ w_out

def second_inputs(seed: int = 0) -> dict:
    key = jax.random.key(seed)
    ks = jax.random.split(key, 32)
    D = D_MODEL

    def nrm(i, shape, scale):
        return scale * jax.random.normal(ks[i], shape, jnp.float32)

    lam_a = jax.random.uniform(ks[13], (N_EVEN, RG_WIDTH), jnp.float32, 0.9, 0.999)
    lam_root = lam_a ** (1.0 / RG_C)
    ev_lam = jnp.log(lam_root) - jnp.log1p(-lam_root)
    return {
        "x": nrm(0, (BATCH, SEQ, D), 1.0),
        "c": nrm(1, (BATCH, D), 1.0),
        "ada_w": nrm(2, (DEPTH, 2, D, 3 * D), 0.1 * D ** -0.5),
        "ada_b": nrm(3, (DEPTH, 2, 3 * D), 0.02),
        "ln_g": 1.0 + nrm(4, (DEPTH, 2, D), 0.05),
        "ln_b": nrm(5, (DEPTH, 2, D), 0.02),
        "ev_w_in": nrm(6, (N_EVEN, D, EVEN_IN), D ** -0.5),
        "ev_conv_w": nrm(7, (N_EVEN, CONV_WIDTH, RG_WIDTH), CONV_WIDTH ** -0.5),
        "ev_conv_b": nrm(8, (N_EVEN, RG_WIDTH), 0.02),
        "ev_rg_wa": nrm(9, (N_EVEN, RG_BLOCKS, RG_BLOCK, RG_BLOCK), RG_BLOCK ** -0.5),
        "ev_rg_ba": nrm(10, (N_EVEN, RG_WIDTH), 0.02),
        "ev_rg_wx": nrm(11, (N_EVEN, RG_BLOCKS, RG_BLOCK, RG_BLOCK), RG_BLOCK ** -0.5),
        "ev_rg_bx": nrm(12, (N_EVEN, RG_WIDTH), 0.02),
        "ev_rg_lam": ev_lam,
        "ev_gla_w_up": nrm(14, (N_EVEN, GLA_LOWRANK, GLA_KDIM), GLA_LOWRANK ** -0.5),
        "ev_gla_b_up": nrm(15, (N_EVEN, GLA_KDIM), 0.02),
        "ev_gla_norm_g": 1.0 + nrm(16, (N_EVEN, GLA_VDIM), 0.05),
        "ev_w_out": nrm(17, (N_EVEN, MIX_WIDTH, D), BETA * MIX_WIDTH ** -0.5),
        "od_w_in": nrm(18, (N_ODD, D, ODD_IN), D ** -0.5),
        "od_b_f": 3.0 + 3.0 * jax.random.uniform(ks[19], (N_ODD, FOX_HEADS), jnp.float32),
        "od_q_norm_g": 1.0 + nrm(20, (N_ODD, FOX_HD), 0.05),
        "od_k_norm_g": 1.0 + nrm(21, (N_ODD, FOX_HD), 0.05),
        "od_w_out": nrm(22, (N_ODD, D, D), BETA * D ** -0.5),
        "mlp_w1": nrm(23, (DEPTH, D, D_FF), D ** -0.5),
        "mlp_b1": nrm(24, (DEPTH, D_FF), 0.02),
        "mlp_w2": nrm(25, (DEPTH, D_FF, D), BETA * D_FF ** -0.5),
        "mlp_b2": nrm(26, (DEPTH, D), 0.02),
    }

def second_block(x, c, ada_w, ada_b, ln_g, ln_b,
              ev_w_in, ev_conv_w, ev_conv_b, ev_rg_wa, ev_rg_ba, ev_rg_wx, ev_rg_bx, ev_rg_lam,
              ev_gla_w_up, ev_gla_b_up, ev_gla_norm_g, ev_w_out,
              od_w_in, od_b_f, od_q_norm_g, od_k_norm_g, od_w_out,
              mlp_w1, mlp_b1, mlp_w2, mlp_b2):
    for layer in range(DEPTH):
        shift, scale, gate = ada_mod(c, ada_w[layer, 0], ada_b[layer, 0])
        u = x * (1.0 + scale) + shift
        if layer % 2 == 0:
            e = layer // 2
            y = even_mixer(u, ev_w_in[e], ev_conv_w[e], ev_conv_b[e], ev_rg_wa[e], ev_rg_ba[e],
                           ev_rg_wx[e], ev_rg_bx[e], ev_rg_lam[e], ev_gla_w_up[e], ev_gla_b_up[e],
                           ev_gla_norm_g[e], ev_w_out[e])
        else:
            o = layer // 2
            y = fox_attention(u, od_w_in[o], od_b_f[o], od_q_norm_g[o], od_k_norm_g[o], od_w_out[o])
        x = layer_norm(ALPHA * x + gate * y, ln_g[layer, 0], ln_b[layer, 0])
        shift, scale, gate = ada_mod(c, ada_w[layer, 1], ada_b[layer, 1])
        u = x * (1.0 + scale) + shift
        y = jnp.square(jax.nn.relu(u @ mlp_w1[layer] + mlp_b1[layer])) @ mlp_w2[layer] + mlp_b2[layer]
        x = layer_norm(ALPHA * x + gate * y, ln_g[layer, 1], ln_b[layer, 1])
    return x


def setup_inputs(seed=0):
    out = dict(first_inputs(seed))
    for name, value in second_inputs(seed + 1).items():
        if name != "x":
            out[name + "_2"] = value
    return out


def reference(
    x, meta_tokens, a_norm, a_w, a_scale, b_norm, b_w_dq, b_q_norm, b_w_uq, b_w_o, kv_norm,
    w_dkv, kv_lat_norm, w_uk, w_uv, ffn_norm, router_g, router_g_bias, router_e, router_e_bias,
    w_gate, w_up, w_down, final_norm, c_2, ada_w_2, ada_b_2, ln_g_2, ln_b_2, ev_w_in_2,
    ev_conv_w_2, ev_conv_b_2, ev_rg_wa_2, ev_rg_ba_2, ev_rg_wx_2, ev_rg_bx_2, ev_rg_lam_2,
    ev_gla_w_up_2, ev_gla_b_up_2, ev_gla_norm_g_2, ev_w_out_2, od_w_in_2, od_b_f_2,
    od_q_norm_g_2, od_k_norm_g_2, od_w_out_2, mlp_w1_2, mlp_b1_2, mlp_w2_2, mlp_b2_2,
):
    x = first_block(
        x, meta_tokens, a_norm, a_w, a_scale, b_norm, b_w_dq, b_q_norm, b_w_uq, b_w_o, kv_norm,
        w_dkv, kv_lat_norm, w_uk, w_uv, ffn_norm, router_g, router_g_bias, router_e,
        router_e_bias, w_gate, w_up, w_down, final_norm,
    )
    return second_block(
        x, c_2, ada_w_2, ada_b_2, ln_g_2, ln_b_2, ev_w_in_2, ev_conv_w_2, ev_conv_b_2,
        ev_rg_wa_2, ev_rg_ba_2, ev_rg_wx_2, ev_rg_bx_2, ev_rg_lam_2, ev_gla_w_up_2,
        ev_gla_b_up_2, ev_gla_norm_g_2, ev_w_out_2, od_w_in_2, od_b_f_2, od_q_norm_g_2,
        od_k_norm_g_2, od_w_out_2, mlp_w1_2, mlp_b1_2, mlp_w2_2, mlp_b2_2,
    )


_drawn_inputs = setup_inputs


def setup_inputs(seed=0):
    import zlib

    import numpy as np

    out = dict(_drawn_inputs(seed))
    spreads = {}
    factors = {'b_norm': 5.401,
     'b_q_norm': 5.091,
     'kv_norm': 3.217,
     'kv_lat_norm': 3.559,
     'router_g_bias': 4.789,
     'ev_conv_b_2': 3.733,
     'ev_rg_ba_2': 64.0,
     'ev_rg_bx_2': 35.915,
     'ev_gla_w_up_2': 3.919,
     'ev_gla_b_up_2': 8.0,
     'ev_gla_norm_g_2': 6.846,
     'od_b_f_2': 38.208,
     'od_q_norm_g_2': 8.0,
     'od_k_norm_g_2': 8.0,
     'mlp_b1_2': 4.284,
     'mlp_b2_2': 2.949}
    for name, (base, spread) in spreads.items():
        noise = np.random.default_rng([zlib.crc32(name.encode()), seed]).standard_normal(out[name].shape)
        drawn = base * np.exp(spread * noise) if base else spread * noise
        out[name] = __import__('jax').numpy.asarray(drawn.astype(out[name].dtype))
    for name, factor in factors.items():
        out[name] = (out[name] * factor).astype(out[name].dtype)
    return out
```

```python
import concourse.bass as bass
from concourse import mybir
from contextlib import ExitStack

F32 = mybir.dt.float32
F32R = mybir.dt.float32r
I32 = mybir.dt.int32
ALU = mybir.AluOpType
ACT = mybir.ActivationFunctionType
AX = mybir.AxisListType

P = 128
D = 1024
DK = D // P
SEQ, META = 512, 16
XT = SEQ // P
KEYS = SEQ + META
CW = 2048
RAW_SLOTS, SPLIT_SLOTS = 4, 3
LOOK = SPLIT_SLOTS - 1
HALF = 512
RMS_EPS, LN_EPS = 1e-6, 1e-5
ALPHA = 4.0 ** 0.25
NE, NG, EPG, DE = 32, 4, 8, 256
NBLK = 40
TABW = NBLK + 2
BODY = 4
BIG = 1e30
HEADS, NOPE, ROPE, VD = 8, 128, 64, 128
QR, KVR = 384, 256
MLA_SCALE = (NOPE + ROPE) ** -0.5
FOX_HD = 64
EPSCOL, LNEPSCOL, ONECOL = 0, 1, 2


class Progress:

    def __init__(self, sem, key, marks):
        self.sem, self.key, self.marks, self.n = sem, key, marks, 0
        self.i, self.base = None, 0

    def step(self, *label, by=1):
        self.n += by
        if label:
            self.mark(*label)
        return self.sem, by

    def mark(self, *label):
        self.marks[label] = (self.key, self.n, None if self.i is None else ("stride", self.key, self.base))

    def stride(self):
        return self.marks.get(("stride", self.key, self.base), 0)

    def now(self):
        return self.sem, (self.n if self.i is None else self.n + self.i * self.stride())

    def enter(self, i):
        self.i, self.base = i, self.n

    def leave(self, rounds):
        k = self.n - self.base
        self.marks[("stride", self.key, self.base)] = k
        self.n, self.i = self.base + k * rounds, None


class Kernel:

    def __init__(self, nc, ctx, marks, dram, stop):
        self.nc, self.ctx, self.marks, self.dram, self.stop = nc, ctx, marks, dram, stop
        self.sems = {}
        self.A, self.V, self.T, self.G, self.S = (
            self.counter(n) for n in ("scalar_done", "vector_done", "tensor_done", "gpsimd_done", "sync_done"))

    def counter(self, name):
        if name not in self.sems:
            self.sems[name] = Progress(self.ctx.enter_context(self.nc.semaphore(name)), name, self.marks)
        return self.sems[name]

    def after(self, *label, i=None, lag=0):
        if label not in self.marks:
            assert not self.marks.get("complete"), label
            return self.A.sem, 1
        key, n, loop = self.marks[label]
        p = self.counter(key)
        if i is None:
            return p.sem, n
        k = self.marks.get(loop, 0)
        return p.sem, n - lag * k + i * k

    def at(self, name, shape, offset, dtype=F32):
        size = 4
        for s in shape[1:]:
            size *= s
        assert offset % 32 == 0 and offset + size <= self.nc.sbuf_usable_end, (name, offset, size)
        self.end = offset + (size + 31) // 32 * 32
        return self.nc.alloc_sbuf_tensor_at(name, shape, dtype, offset=offset)


def products(pe, out, ah, al, bh, bl, first, last):
    pe.matmul(out, ah, bh, start=first, stop=False)
    pe.matmul(out, al, bh, start=False, stop=False)
    return pe.matmul(out, ah, bl, start=False, stop=last)


_C = {}
_at = 0
for _name, _w in (("ident", P), ("ones", P), ("upper", P), ("future", P), ("chunkmask", P), ("pairs", P), ("rev", NG + NE),
                  ("valid", XT + 1), ("absent", XT + 1), ("eps", 1), ("lneps", 1), ("one", 1), ("blocks", TABW),
                  ("cos", (XT + 1) * ROPE // 2), ("sin", (XT + 1) * ROPE // 2)):
    _C[_name] = (_at, _w)
    _at += _w
CONSTW = _at
_R = {}
_at = 0
for _name, _w in (("adab", 64), ("c", DK), ("convw", 16), ("convb", 4), ("ba", 4), ("bx", 4), ("lam", 4),
                  ("bup", 2), ("glag", 4), ("foxq", 1), ("foxk", 1), ("bf", 1), ("b1", 64),
                  ("qrow", QR), ("kvrow", KVR), ("rbias", 2 * (NG + NE))):
    _R[_name] = (_at, _w)
    _at += _w
PARAMW = _at

ROWS = ["a_norm", "a_scale", "ffn0", "kv_norm", "b_norm", "ffn1", "final"]
for _s in range(4):
    ROWS += [f"gate{_s}"] + ([f"b2{_s}"] if _s % 2 else []) + [f"lng{_s}", f"lnb{_s}"]
ROW_SLOTS = 3


def const(k, name, rows=P):
    at, w = _C[name]
    return k.CONST[0:rows, at:at + w]


def param(k, name, i=0, n=None, rows=P):
    at, w = _R[name]
    return k.PARAM[0:rows, at + i:at + (w if n is None else i + n)]


def row(k, name, w=D):
    return k.ROWB[:, ROWS.index(name) % ROW_SLOTS, 0:w]


def flat(k, a, b, rows=P):
    return k.PS[0:rows, :, :].rearrange("p a b -> p (a b)")[:, a:b]



def load_chunk(k, sync, c):
    if c >= RAW_SLOTS:
        f = c - RAW_SLOTS
        c0 = next((b for b in k.MOE0 if b <= f < b + 3 * NBLK), None)
        if c0 is None:
            sync.wait_ge(*k.after("raw free", f))
        else:
            i, q = divmod(f - c0, 3 * BODY)
            sync.wait_ge(*k.after("raw free", c0 + q, i=i, lag=1 if q < MOE_LOOK else 0))
    src, w = k.CH[c]
    sync.dma_start(k.RAW[c % RAW_SLOTS][:, 0:w], src).then_inc(
        *k.counter(f"raw{c % RAW_SLOTS}_loaded").step("raw", c, by=16))


def split_high(k, act, upto):
    while k.high_next <= min(upto, len(k.CH) - 1) and k.high_next not in k.MOE0:
        c = k.high_next
        k.high_next += 1
        if not k.SPLIT[c]:
            continue
        s = k.SPLIT_NO[c]
        act.wait_ge(*k.after("raw", c))
        if s >= SPLIT_SLOTS:
            act.wait_ge(*k.after("used", s - SPLIT_SLOTS))
        w = k.CH[c][1]
        act.activation(k.WH[s % SPLIT_SLOTS][:, 0:w], k.RAW[c % RAW_SLOTS][:, 0:w], ACT.Copy).then_inc(
            *k.A.step("high", c))


def split_low(k, dve, upto):
    while k.low_next <= min(upto, len(k.CH) - 1) and k.low_next not in k.MOE0 and k.SPLIT[k.low_next]:
        c = k.low_next
        k.low_next += 1
        s = k.SPLIT_NO[c]
        dve.wait_ge(*k.after("raw", c))
        dve.wait_ge(*k.after("high", c))
        if s >= SPLIT_SLOTS:
            dve.wait_ge(*k.after("used", s - SPLIT_SLOTS))
        w = k.CH[c][1]
        dve.tensor_tensor(k.WL[s % SPLIT_SLOTS][:, 0:w], k.RAW[c % RAW_SLOTS][:, 0:w],
                          k.WH[s % SPLIT_SLOTS][:, 0:w].bitcast(F32), ALU.subtract).then_inc(*k.V.step("low", c))
        k.V.mark("raw free", c)


def chunk_pair(k, pe, c):
    pe.wait_ge(*k.after("high", c))
    pe.wait_ge(*k.after("low", c))
    s = k.SPLIT_NO[c] % SPLIT_SLOTS
    return k.WH[s], k.WL[s]



def tile_col(t):
    return (t * P, P) if t < XT else (SEQ, META)


def norm_scalar(k, act, name, tiles, mode):
    for t in tiles:
        act.wait_ge(*k.A.now())
        act.activation(k.SQ[:, :], k.H[:, t, :], ACT.Square, accum_out=k.SS[:, t:t + 1]).then_inc(*k.A.step())
    act.wait_ge(*k.A.now())
    n = len(tiles)
    act.activation(k.RT[:, 0:n], k.SS[:, 0:n], ACT.Sqrt, scale=1.0 / D, bias=const(k, "eps")).then_inc(
        *k.A.step(name, "root"))
    for t in tiles if mode else []:
        c0, w = tile_col(t)
        for half in range(2):
            b = (2 * t + half) % 4
            src = k.PS[:, b, :].rearrange("p (a c) -> p a c", a=4)
            act.wait_ge(*k.after(name, "turned", t, half))
            rows = slice(4 * half, 4 * half + 4)
            if mode == "pair":
                act.activation(k.XH[:, rows, c0:c0 + w], src[:, :, 0:w], ACT.Copy).then_inc(
                    *k.A.step(name, "hi", t, half))
            elif mode == "pool":
                c0, w = (2 * META + t * P, P) if t < XT else (META, META)
                act.activation(k.XP[:, rows, c0:c0 + w], src[:, :, 0:w], ACT.Copy).then_inc(
                    *k.A.step(name, "out", t, half))
            else:
                if t >= 2:
                    act.wait_ge(*k.after(name, "logits", t - 2))
                act.activation(k.XF[:, t % 2, rows, :], src, ACT.Copy).then_inc(*k.A.step(name, "out", t, half))


def norm_vector(k, dve, name, tiles, mode, gain):
    n = len(tiles)
    dve.wait_ge(*k.after(name, "root"))
    dve.reciprocal(k.RS[:, 0:n], k.RT[:, 0:n]).then_inc(*k.V.step())
    dve.wait_ge(*k.V.now())
    dve.wait_ge(*k.after("row", gain))
    def lows(t):
        c0, w = tile_col(t)
        for half in range(2):
            b = (2 * t + half) % 4
            src = k.PS[:, b, :].rearrange("p (a c) -> p a c", a=4)
            rows = slice(4 * half, 4 * half + 4)
            dve.wait_ge(*k.after(name, "hi", t, half))
            dve.tensor_tensor(k.XL[:, rows, c0:c0 + w], src[:, :, 0:w], k.XH[:, rows, c0:c0 + w].bitcast(F32),
                              ALU.subtract).then_inc(*k.V.step(name, "out", t, half))
    for t in tiles:
        if t >= 2:
            dve.wait_ge(*k.after(name, "turned", t - 2, 1))
            if mode == "router":
                dve.wait_ge(*k.after(name, "stored", t - 2))
        dve.scalar_tensor_tensor(out=k.XN[:, t % 2, :], in0=k.H[:, t, :], scalar=k.RS[:, t:t + 1], in1=row(k, gain),
                                 op0=ALU.mult, op1=ALU.mult).then_inc(*k.V.step(name, "xn", t))
        if mode == "pair" and t >= 1:
            lows(t - 1)
    k.V.mark("row done", gain)
    if mode == "pair":
        lows(tiles[-1])


def norm_tensor(k, pe, name, tiles):
    for t in tiles:
        pe.wait_ge(*k.after(name, "xn", t))
        for half in range(2):
            b = (2 * t + half) % 4
            if t >= 2:
                pe.wait_ge(*k.after(name, "out", t - 2, half))
            for i in range(4):
                j = 4 * half + i
                mm = pe.transpose(k.PS[:, b, i * P:(i + 1) * P], k.XN[:, t % 2, j * P:(j + 1) * P], const(k, "ident"))
            mm.then_inc(*k.T.step(name, "turned", t, half))
        if name in ("route0", "route1"):
            logits_tensor(k, pe, name, t)



POOL_G = D // 4


def load_counts(k, sync):
    sync.dma_start(k.RC[:, :, :], k.dram["rcnt"]).then_inc(*k.counter("rcnt_loaded").step("rcnt", by=16))


def pool_gpsimd(k, pool):
    load_counts(k, pool)
    pool.memset(k.XP[:, :, 0:META], 0.0).then_inc(*k.G.step())
    pool.memset(k.PA[:, :, :], 0.0).then_inc(*k.G.step())
    pool.memset(k.PB[:, :, :], 0.0).then_inc(*k.G.step("pads"))


def pool_scalar(k, act):
    norm_scalar(k, act, "pool", range(XT + 1), "pool")
    split_high(k, act, LOOK)
    for g in range(4):
        act.wait_ge(*k.after("pooled", g))
        act.activation(k.XH[:, 2 * g:2 * g + 2, 0:SEQ], k.PL[:, :, META:KEYS], ACT.Copy).then_inc(*k.A.step())
        act.activation(k.XH[:, 2 * g:2 * g + 2, SEQ:KEYS], k.PL[:, :, 0:META], ACT.Copy).then_inc(
            *k.A.step("pool hi", g))


def pool_vector(k, dve):
    norm_vector(k, dve, "pool", range(XT + 1), "pool", "a_norm")
    split_low(k, dve, LOOK)
    dve.wait_ge(*k.after("pads"))
    dve.wait_ge(*k.after("rcnt"))
    dve.wait_ge(*k.after("pool", "out", XT, 1))
    for g in range(4):
        rows = slice(2 * g, 2 * g + 2)
        x = k.XP[:, rows, :]
        cur = x
        for level in range(g + 1):
            nxt = (k.PA, k.PB)[level % 2]
            d = 1 << level
            dve.wait_ge(*k.V.now())
            dve.tensor_tensor(nxt[:, :, META:META + KEYS], cur[:, :, META:META + KEYS],
                              cur[:, :, META - d:META - d + KEYS], ALU.add).then_inc(*k.V.step())
            cur = nxt
        dve.wait_ge(*k.V.now())
        out = (k.PA, k.PB)[(g + 1) % 2]
        dve.tensor_tensor(out[:, :, META:META + KEYS], cur[:, :, META:META + KEYS],
                          k.RC[:, g:g + 1, :].to_broadcast([P, 2, KEYS]), ALU.mult).then_inc(*k.V.step())
        dve.wait_ge(*k.V.now())
        if g:
            dve.wait_ge(*k.after("pool hi", g - 1))
        dve.tensor_tensor(k.PL[:, :, :], out[:, :, META:META + KEYS], x[:, :, META:META + KEYS],
                          ALU.subtract).then_inc(*k.V.step("pooled", g))
        dve.wait_ge(*k.V.now())
        dve.wait_ge(*k.after("pool hi", g))
        for a, b, c in ((0, SEQ, META), (SEQ, KEYS, 0)):
            dve.tensor_tensor(k.XL[:, rows, a:b], k.PL[:, :, c:c + b - a], k.XH[:, rows, a:b].bitcast(F32),
                              ALU.subtract).then_inc(*k.V.step())
        k.V.mark("pool lo", g)
    dve.wait_ge(*k.after("row", "a_scale"))
    for t in range(XT + 1):
        n = tile_col(t)[1]
        for half in range(2):
            b = (2 * t + half) % 4 + 4
            dve.wait_ge(*k.after("mixed", t, half))
            dve.wait_ge(*k.V.now())
            cols = slice(half * HALF, half * HALF + HALF)
            dve.tensor_tensor(k.TMP[0:n, 0, :], k.PS[0:n, b, :], row(k, "a_scale")[0:n, cols], ALU.mult).then_inc(
                *k.V.step("mix out", t, half))
            dve.wait_ge(*k.V.now())
            dve.tensor_tensor(k.H[0:n, t, cols], k.H[0:n, t, cols], k.TMP[0:n, 0, :], ALU.add).then_inc(*k.V.step())
    k.V.mark("row done", "a_scale")


def pool_tensor(k, pe):
    norm_tensor(k, pe, "pool", range(XT + 1))
    wh, wl = chunk_pair(k, pe, 0)
    pe.wait_ge(*k.after("pool lo", 3))
    for t in range(XT + 1):
        c0, n = tile_col(t)
        for half in range(2):
            b = (2 * t + half) % 4 + 4
            if t >= 2:
                pe.wait_ge(*k.after("mix out", t - 2, half))
            for g in (2 * half, 2 * half + 1):
                for j in range(2):
                    w = slice((2 * g + j) * POOL_G, (2 * g + j + 1) * POOL_G)
                    mm = products(pe, k.PS[0:n, b, (g % 2) * POOL_G:(g % 2 + 1) * POOL_G],
                                  k.XH[:, 2 * g + j, c0:c0 + n], k.XL[:, 2 * g + j, c0:c0 + n],
                                  wh[:, w], wl[:, w], j == 0, j == 1)
            mm.then_inc(*k.T.step("mixed", t, half))
    k.T.mark("used", 0)



def logits_tensor(k, pe, name, t):
    pe.wait_ge(*k.after(name, "out", t, 0))
    pe.wait_ge(*k.after(name, "out", t, 1))
    pe.wait_ge(*k.after("router weights", name[-1]))
    w = NG + NE
    for j in range(DK):
        mm = pe.matmul(k.PS[:, 4, t * w:(t + 1) * w], k.XF[:, t % 2, j, :], k.WR[:, j, :], start=(j == 0), stop=(j == DK - 1))
    mm.then_inc(*k.T.step(name, "logits", t))


def route_tensor(k, pe, L, T):
    norm_tensor(k, pe, f"route{L}", range(T))
    pe.wait_ge(*k.after("picked", L))
    for t in range(T):
        out = k.PS[:, 5, t * NE:(t + 1) * NE]
        for u in range(t):
            pe.matmul(out, const(k, "ones"), k.PICK[:, u, :], start=(u == 0), stop=False)
        mm = pe.matmul(out, const(k, "upper"), k.PICK[:, t, :], start=(t == 0), stop=True)
    for t in range(T):
        mm = pe.matmul(k.PS[:, 6, 0:NE], const(k, "ones"), k.PICK[:, t, :], start=(t == 0), stop=(t == T - 1))
    mm.then_inc(*k.T.step("ranked", L))


def route_scalar(k, act, L, T):
    norm_scalar(k, act, f"route{L}", range(T), "router")
    act.wait_ge(*k.after("group logits", L))
    act.activation(k.EG[:, 0:T, :], k.DG[:, 0:T, :], ACT.Exp).then_inc(*k.A.step("group exp", L))
    act.wait_ge(*k.after("gap", L))
    act.activation(k.E2[:, 0:T], k.GAP[:, 0:T], ACT.Exp).then_inc(*k.A.step("gap exp", L))


def first_of(k, dve, hit, at_max, rev, best, T, w):
    dve.wait_ge(*k.V.now())
    dve.tensor_tensor(hit, at_max, rev, ALU.mult).then_inc(*k.V.step())
    dve.wait_ge(*k.V.now())
    dve.tensor_reduce(best, hit, AX.X, ALU.max).then_inc(*k.V.step())
    dve.wait_ge(*k.V.now())
    dve.tensor_tensor(hit, hit, best.unsqueeze(2).to_broadcast([P, T, w]), ALU.is_equal).then_inc(*k.V.step())
    dve.wait_ge(*k.V.now())


def route_vector(k, dve, L, T):
    name = f"route{L}"
    norm_vector(k, dve, name, range(T), "router", f"ffn{L}")
    w = NG + NE
    V = k.V
    def bc(a, n):
        return a.unsqueeze(2).to_broadcast([P, T, n])
    dve.wait_ge(*k.after(name, "logits", T - 1))
    lg = k.LG[:, 0:T, :]
    at, _ = _R["rbias"]
    bias = k.PARAM[:, at + L * w:at + (L + 1) * w].unsqueeze(1).to_broadcast([P, T, w])
    dve.tensor_tensor(lg, k.PS[:, 4, 0:T * w].rearrange("p (t w) -> p t w", t=T), bias, ALU.add).then_inc(*V.step())
    dve.wait_ge(*V.now())
    m, best = k.RM[:, 0, 0:T], k.RM[:, 1, 0:T]
    dg, g1h = k.DG[:, 0:T, :], k.G1H[:, 0:T, :]
    dve.tensor_reduce(m, lg[:, :, 0:NG], AX.X, ALU.max).then_inc(*V.step())
    dve.tensor_copy(k.LE[:, 0:T, :], lg[:, :, NG:w]).then_inc(*V.step())
    dve.wait_ge(*V.now())
    dve.tensor_tensor(dg, lg[:, :, 0:NG], bc(m, NG), ALU.subtract).then_inc(*V.step("group logits", L))
    dve.wait_ge(*V.now())
    dve.tensor_scalar(g1h, dg, 0.0, None, ALU.is_ge).then_inc(*V.step())
    at, _ = _C["rev"]
    first_of(k, dve, g1h, g1h, k.CONST[:, at:at + NG].unsqueeze(1).to_broadcast([P, T, NG]), best, T, NG)
    dve.tensor_scalar(k.PEN[:, 0:T, :], g1h, -1.0, BIG, ALU.add, ALU.mult).then_inc(*V.step())
    dve.wait_ge(*V.now())
    le4 = k.LE[:, 0:T, :].rearrange("p t (g e) -> p (t g) e", g=NG)
    pen4 = k.PEN[:, 0:T, :].rearrange("p t g -> p (t g)").unsqueeze(2).to_broadcast([P, T * NG, EPG])
    dve.tensor_tensor(le4, le4, pen4, ALU.add).then_inc(*V.step())
    le = k.LE[:, 0:T, :]
    rev = k.CONST[:, at + NG:at + w].unsqueeze(1).to_broadcast([P, T, NE])
    for n, hit in enumerate((k.HIT1[:, 0:T, :], k.HIT2[:, 0:T, :])):
        top = k.RM[:, 2 + n, 0:T]
        dve.wait_ge(*V.now())
        dve.tensor_reduce(top, le, AX.X, ALU.max).then_inc(*V.step())
        dve.wait_ge(*V.now())
        dve.tensor_tensor(hit, le, bc(top, NE), ALU.is_equal).then_inc(*V.step())
        first_of(k, dve, hit, hit, rev, best, T, NE)
        if n == 0:
            dve.scalar_tensor_tensor(out=le, in0=hit, scalar=-BIG, in1=le, op0=ALU.mult, op1=ALU.add).then_inc(*V.step())
    dve.tensor_tensor(k.PICK[:, 0:T, :], k.HIT1[:, 0:T, :], k.HIT2[:, 0:T, :], ALU.add).then_inc(*V.step())
    dve.tensor_tensor(k.GAP[:, 0:T], k.RM[:, 3, 0:T], k.RM[:, 2, 0:T], ALU.subtract).then_inc(*V.step("gap", L))
    dve.wait_ge(*V.now())
    at, _ = _C["valid"]
    dve.tensor_tensor(k.PICK[:, 0:T, :], k.PICK[:, 0:T, :], bc(k.CONST[:, at:at + T], NE), ALU.mult).then_inc(
        *V.step("picked", L))
    dve.wait_ge(*k.after("group exp", L))
    dve.tensor_reduce(k.RM[:, 4, 0:T], k.EG[:, 0:T, :], AX.X, ALU.add).then_inc(*V.step())
    dve.wait_ge(*k.after("gap exp", L))
    dve.tensor_scalar(k.RM[:, 5, 0:T], k.E2[:, 0:T], 1.0, None, ALU.add).then_inc(*V.step())
    dve.wait_ge(*V.now())
    dve.tensor_tensor(k.RM[:, 4, 0:T], k.RM[:, 4, 0:T], k.RM[:, 5, 0:T], ALU.mult).then_inc(*V.step())
    dve.wait_ge(*V.now())
    dve.reciprocal(k.GATE[:, 0, 0:T], k.RM[:, 4, 0:T]).then_inc(*V.step())
    dve.wait_ge(*V.now())
    dve.tensor_tensor(k.GATE[:, 1, 0:T], k.GATE[:, 0, 0:T], k.E2[:, 0:T], ALU.mult).then_inc(*V.step())
    dve.wait_ge(*k.after("ranked", L))
    cnt, nb, end = k.CNT[:, 0, :], k.CNT[:, 1, :], k.CNT[:, 2, :]
    dve.tensor_copy(cnt, k.PS[:, 6, 0:NE]).then_inc(*V.step())
    dve.wait_ge(*V.now())
    dve.tensor_scalar(nb, cnt, 0.0, None, ALU.is_gt).then_inc(*V.step())
    for j in range(1, T):
        dve.wait_ge(*V.now())
        dve.scalar_tensor_tensor(out=nb, in0=cnt, scalar=float(P * j), in1=nb, op0=ALU.is_gt, op1=ALU.add).then_inc(*V.step())
    dve.wait_ge(*V.now())
    dve.tensor_tensor_scan(end, const(k, "ones")[:, 0:NE], nb, 0.0, ALU.mult, ALU.add).then_inc(*V.step())
    dve.wait_ge(*V.now())
    dve.tensor_tensor(nb, end, nb, ALU.subtract).then_inc(*V.step())
    pos = k.POS[:, 0:T, :]
    pb = k.LE[:, 0:T, :]
    dve.tensor_copy(pos, k.PS[:, 5, 0:T * NE].rearrange("p (t w) -> p t w", t=T)).then_inc(*V.step())
    dve.wait_ge(*V.now())
    dve.tensor_scalar(pb, pos, float(P), None, ALU.is_ge).then_inc(*V.step())
    for j in range(2, T):
        dve.wait_ge(*V.now())
        dve.scalar_tensor_tensor(out=pb, in0=pos, scalar=float(P * j), in1=pb, op0=ALU.is_ge, op1=ALU.add).then_inc(*V.step())
    dve.wait_ge(*V.now())
    dve.tensor_scalar(pos, pos, float(TABW), None, ALU.mult).then_inc(*V.step())
    dve.wait_ge(*V.now())
    dve.scalar_tensor_tensor(out=pos, in0=pb, scalar=float(1 - P * TABW), in1=pos, op0=ALU.mult, op1=ALU.add).then_inc(*V.step())
    dve.wait_ge(*V.now())
    dve.tensor_tensor(pos, pos, nb.unsqueeze(1).to_broadcast([P, T, NE]), ALU.add).then_inc(*V.step())
    at, _ = _C["absent"]
    for n, hit in enumerate((k.HIT1[:, 0:T, :], k.HIT2[:, 0:T, :])):
        dve.wait_ge(*V.now())
        dve.tensor_tensor(hit, hit, pos, ALU.mult).then_inc(*V.step())
        dve.wait_ge(*V.now())
        dve.tensor_reduce(k.RM[:, 6 + n, 0:T], hit, AX.X, ALU.add).then_inc(*V.step())
        dve.wait_ge(*V.now())
        dve.tensor_tensor(k.DEST[:, n, 0:T], k.RM[:, 6 + n, 0:T], k.CONST[:, at:at + T], ALU.add).then_inc(*V.step("dest", L, n))
    at, _ = _C["blocks"]
    dve.tensor_tensor(k.CMP[0:1, :, :], k.CONST[0:1, at:at + TABW].unsqueeze(2).to_broadcast([1, TABW, NE]),
                      end[0:1, :].unsqueeze(1).to_broadcast([1, TABW, NE]), ALU.is_ge).then_inc(*V.step())
    dve.wait_ge(*V.now())
    dve.tensor_reduce(k.BE[0:1, :], k.CMP[0:1, :, :], AX.X, ALU.add).then_inc(*V.step())
    dve.wait_ge(*V.now())
    dve.tensor_scalar(k.BE[0:1, :], k.BE[0:1, :], float(NE - 1), 3.0, ALU.min, ALU.mult).then_inc(*V.step())
    dve.wait_ge(*V.now())
    dve.tensor_scalar(k.BEI[0:1, :], k.BE[0:1, :], float(3 * NE * L), None, ALU.add).then_inc(*V.step("experts", L))


def store_rows(k, sync, L, T):
    sync.dma_start(k.WR[:, :, :], k.dram["wr"][L]).then_inc(*k.counter(f"router{L}_loaded").step("router weights", str(L), by=16))
    for t in range(T):
        sync.wait_ge(*k.after(f"route{L}", "xn", t))
        sync.dma_start(k.xn_d[t * P:(t + 1) * P, :], k.XN[:, t % 2, :]).then_inc(
            *k.counter(f"xn_stored{t % 2}").step(f"route{L}", "stored", t, by=16))


def route_gpsimd(k, pool, L, T):
    store_rows(k, pool, L, T)
    if L:
        pool.wait_ge(*k.after("table read", L - 1))
    pool.dma_start(k.tab_d.rearrange("(p b) c -> p (b c)", p=P), k.TABI[:, :]).then_inc(
        *k.counter("table_blank").step("blank", L, by=16))
    pool.wait_ge(*k.after("blank", L))
    for t in range(T):
        for n in range(2):
            pool.wait_ge(*k.after("dest", L, n))
            pool.indirect_dma_start(
                k.tab_d[:, :], bass.IndirectOffsetOnAxis(ap=k.DEST[:, n, t:t + 1], axis=0),
                k.AID[:, 2 * (2 * t + n):2 * (2 * t + n) + 2], None, bounds_check=P * TABW - 1,
                oob_is_err=False).then_inc(*k.counter("table_filled").step("filled", L, t, n, by=16))
    pool.wait_ge(*k.after("filled", L, T - 1, 1))
    pool.dma_start(k.TAB[:, :], k.tab_d.rearrange("(p b) c -> p (b c)", p=P)).then_inc(
        *k.counter("table_loaded").step("table read", L, by=16))
    pool.wait_ge(*k.after("table read", L))
    for t in range(T):
        pool.wait_ge(*k.after(f"route{L}", "stored", t))



def moe_sync(k, sync, L, c0):
    raws = [k.counter(f"raw{s}_loaded") for s in range(RAW_SLOTS)]
    sync.wait_ge(*k.after("experts", L))
    sync.wait_ge(*k.after("raw free", c0 - 1))
    with sync.Fori(0, NBLK // BODY) as i:
        for r in raws:
            r.enter(i)
        for j in range(BODY):
            e = sync.value_load(k.BEI[0:1, bass.ds(i * BODY + j, 1)], min_val=0, max_val=2 * 3 * NE - 3)
            for p in range(3):
                q = 3 * j + p
                f = q - RAW_SLOTS
                if 0 <= f < MOE_LOOK:
                    sync.wait_ge(*k.after("moe prologue low", L))
                sync.wait_ge(*k.after("raw free", c0 + f % 12, i=i, lag=(1 if f < MOE_LOOK else 0)))
                sync.dma_start(k.RAW[(c0 + q) % RAW_SLOTS][:, :],
                               k.dram["moe"][bass.ds(e + p, 1), :, :].rearrange("o p m -> (o p) m")).then_inc(
                    *raws[(c0 + q) % RAW_SLOTS].step("raw", c0 + q, by=16))
        for r in raws:
            r.leave(NBLK // BODY)


MOE_LOOK = 3
MOE_SLOTS = 4


def moe_slot(k, c0, q):
    n = q % MOE_SLOTS
    return (k.WHX, k.WLX) if n == SPLIT_SLOTS else (k.WH[(k.SPLIT_NO[c0] + n) % SPLIT_SLOTS], k.WL[(k.SPLIT_NO[c0] + n) % SPLIT_SLOTS])


def loop_high(k, act, c0, q, i):
    lag = -(q // 12)
    q = q % 12
    act.wait_ge(*k.after("raw", c0 + q, i=i, lag=lag))
    u = q - MOE_SLOTS
    act.wait_ge(*k.after("used", k.SPLIT_NO[c0] + u % 12, i=i, lag=lag + (1 if u <= 0 else 0)))
    act.activation(moe_slot(k, c0, q)[0][:, :], k.RAW[(c0 + q) % RAW_SLOTS][:, :], ACT.Copy).then_inc(*k.A.step("high", c0 + q))


def loop_low(k, dve, c0, q, i):
    lag = -(q // 12)
    q = q % 12
    wh, wl = moe_slot(k, c0, q)
    dve.wait_ge(*k.after("raw", c0 + q, i=i, lag=lag))
    dve.wait_ge(*k.after("high", c0 + q, i=i, lag=0))
    u = q - MOE_SLOTS
    dve.wait_ge(*k.after("used", k.SPLIT_NO[c0] + u % 12, i=i, lag=lag + (1 if u <= 0 else 0)))
    dve.tensor_tensor(wl[:, :], k.RAW[(c0 + q) % RAW_SLOTS][:, :], wh[:, :].bitcast(F32), ALU.subtract).then_inc(
        *k.V.step("low", c0 + q))
    k.V.mark("raw free", c0 + q)


def loop_pair(k, pe, c0, q, i):
    lag = 1 if q < MOE_LOOK else 0
    q = q % (3 * BODY)
    pe.wait_ge(*k.after("high", c0 + q, i=i, lag=lag))
    pe.wait_ge(*k.after("low", c0 + q, i=i, lag=lag))
    return moe_slot(k, c0, q)


def moe_tensor(k, pe, L, c0):
    s0 = k.SPLIT_NO[c0]
    T = k.T
    pe.wait_ge(*k.after("moe prologue high", L))
    pe.wait_ge(*k.after("moe prologue low", L))

    def turn(slot, labels):
        for f in range(DK):
            mm = pe.transpose(flat(k, f * P, f * P + P), k.XG[:, slot, f * P:(f + 1) * P], const(k, "ident"))
            if f == 3:
                mm.then_inc(*T.step(*labels[0]))
        mm.then_inc(*T.step(*labels[1]))

    def gate_up(j, p, wh, wl):
        for f in range(4):
            w = slice(f * HALF, f * HALF + HALF)
            mm = products(pe, k.PS[:, 2 + 4 * (j % 2), :], k.XGH[j % 2][:, 4 * p + f, :], k.XGL[j % 2][:, 4 * p + f, :],
                          wh[:, w], wl[:, w], p == 0 and f == 0, p == 1 and f == 3)
        return mm
    pe.wait_ge(*k.after("first gathered", L))
    turn(0, [("first turned", L, half) for half in range(2)])
    pe.wait_ge(*k.after("first x lo", L))
    gate_up(0, 0, *moe_slot(k, c0, 0)).then_inc(*T.step("first gate up", L))
    with pe.Fori(0, NBLK // BODY) as i:
        T.enter(i)
        for j in range(BODY):
            n = (j + 1) % BODY
            prev = dict(i=i, lag=0 if j else 1)
            pe.wait_ge(*k.after("gathered", L, n, i=i, lag=0 if j else 1))
            pe.wait_ge(*k.after("moe x lo", L, j, **prev))
            turn(n % 2, [("moe turned", L, n, half) for half in range(2)])
            gate_up(j, 1, *loop_pair(k, pe, c0, 3 * j + 1, i)).then_inc(*T.step("used", s0 + 3 * j + 1))
            T.mark("gate up", L, j)
            pe.wait_ge(*k.after("moe x lo", L, n, i=i))
            pe.wait_ge(*k.after("hidden", L, (j - 1) % BODY, **prev))
            gate_up(n, 0, *loop_pair(k, pe, c0, 3 * j + 3, i)).then_inc(*T.step("used", s0 + 3 * n))
            pe.wait_ge(*k.after("hidden", L, j, i=i))
            pe.wait_ge(*k.after("hidden lo", L, (j - 1) % BODY, **prev))
            for f in range(2):
                mm = pe.transpose(k.PS[:, 3, f * P:(f + 1) * P], k.HID[:, f * P:(f + 1) * P], const(k, "ident"))
            mm.then_inc(*T.step("hidden turned", L, j))
            pe.wait_ge(*k.after("hidden lo", L, j, i=i))
            pe.wait_ge(*k.after("moe y", L, (j - 1) % BODY, 0, **prev))
            pe.wait_ge(*k.after("moe y", L, (j - 1) % BODY, 1, **prev))
            wh, wl = loop_pair(k, pe, c0, 3 * j + 2, i)
            for half in range(2):
                for f in range(2):
                    w = slice(f * D + half * HALF, f * D + half * HALF + HALF)
                    mm = products(pe, k.PS[:, 4 + half, :], k.HTH[:, f, :], k.HTL[:, f, :], wh[:, w], wl[:, w], f == 0, f == 1)
            mm.then_inc(*T.step("used", s0 + 3 * j + 2))
            T.mark("down", L, j)
        T.leave(NBLK // BODY)
    pe.matmul(k.PS[:, 2, :], k.XGH[0][:, 0, :], moe_slot(k, c0, 0)[0][:, 0:HALF], start=False, stop=True).then_inc(*T.step())
    for q in range(SPLIT_SLOTS):
        T.mark("used", s0 + 3 * NBLK - SPLIT_SLOTS + q)


def moe_scalar(k, act, L, c0):
    A = k.A
    split_high(k, act, c0 - 1)
    act.wait_ge(*k.after("used", k.SPLIT_NO[c0] - 1))
    for q in range(MOE_LOOK):
        act.wait_ge(*k.after("raw", c0 + q, i=0))
        act.activation(moe_slot(k, c0, q)[0][:, :], k.RAW[(c0 + q) % RAW_SLOTS][:, :], ACT.Copy).then_inc(
            *A.step("moe prologue high", L))

    def x_high(slot, half, *label):
        act.activation(k.XGH[slot][:, 4 * half:4 * half + 4, :].rearrange("p a b -> p (a b)"), k.PS[:, half, :],
                       ACT.Copy).then_inc(*A.step(*label))
    for half in range(2):
        act.wait_ge(*k.after("first turned", L, half))
        x_high(0, half, "first x hi", L, half)
    act.wait_ge(*k.after("first gate up", L))
    with act.Fori(0, NBLK // BODY) as i:
        A.enter(i)
        for j in range(BODY):
            n = (j + 1) % BODY
            prev = dict(i=i, lag=0 if j else 1)
            for half in range(2):
                act.wait_ge(*k.after("moe turned", L, n, half, i=i))
                x_high(n % 2, half, "moe x hi", L, n, half)
            loop_high(k, act, c0, 3 * j + 3, i)
            act.wait_ge(*k.after("gate up", L, j, i=i))
            act.wait_ge(*k.after("hidden", L, (j - 1) % BODY, **prev))
            act.activation(k.SILU[:, :], k.PS[:, 2 + 4 * (j % 2), 0:DE], ACT.Silu).then_inc(*A.step("silu", L, j))
            loop_high(k, act, c0, 3 * j + 4, i)
            act.wait_ge(*k.after("hidden turned", L, j, i=i))
            act.wait_ge(*k.after("down", L, (j - 1) % BODY, **prev))
            act.activation(k.HTH[:, :, :].rearrange("p a b -> p (a b)"), k.PS[:, 3, 0:DE], ACT.Copy).then_inc(
                *A.step("hidden hi", L, j))
            loop_high(k, act, c0, 3 * j + 5, i)
            act.wait_ge(*k.after("down", L, j, i=i))
            act.wait_ge(*k.after("scattered", L, (j - 2) % BODY, i=i, lag=0 if j >= 2 else 1))
            act.activation(k.YB[:, j % 2, 0:HALF], k.PS[:, 4, :], ACT.Copy).then_inc(*A.step("moe y", L, j, 0))
        A.leave(NBLK // BODY)
    k.high_next = c0 + 3 * NBLK + MOE_LOOK
    for q in range(MOE_LOOK):
        A.mark("high", c0 + 3 * NBLK + q)


def moe_vector(k, dve, L, c0):
    V = k.V
    split_low(k, dve, c0 - 1)
    dve.wait_ge(*k.after("moe prologue high", L))
    dve.wait_ge(*k.after("used", k.SPLIT_NO[c0] - 1))
    for q in range(MOE_LOOK):
        dve.wait_ge(*k.after("raw", c0 + q, i=0))
        wh, wl = moe_slot(k, c0, q)
        dve.tensor_tensor(wl[:, :], k.RAW[(c0 + q) % RAW_SLOTS][:, :], wh[:, :].bitcast(F32), ALU.subtract).then_inc(
            *V.step("moe prologue low", L))

    def x_low(slot, half, *label):
        dve.tensor_tensor(k.XGL[slot][:, 4 * half:4 * half + 4, :].rearrange("p a b -> p (a b)"), k.PS[:, half, :],
                          k.XGH[slot][:, 4 * half:4 * half + 4, :].rearrange("p a b -> p (a b)").bitcast(F32),
                          ALU.subtract).then_inc(*V.step(*label))
    for half in range(2):
        dve.wait_ge(*k.after("first x hi", L, half))
        x_low(0, half, "first x lo", L)
    dve.wait_ge(*k.after("first gate up", L))
    with dve.Fori(0, NBLK // BODY) as i:
        V.enter(i)
        for j in range(BODY):
            n = (j + 1) % BODY
            prev = dict(i=i, lag=0 if j else 1)
            for half in range(2):
                dve.wait_ge(*k.after("moe x hi", L, n, half, i=i))
                x_low(n % 2, half, "moe x lo", L, n)
            loop_low(k, dve, c0, 3 * j + 3, i)
            dve.wait_ge(*k.after("silu", L, j, i=i))
            dve.wait_ge(*k.after("hidden turned", L, (j - 1) % BODY, **prev))
            dve.tensor_tensor(k.HID[:, :], k.SILU[:, :], k.PS[:, 2 + 4 * (j % 2), DE:2 * DE], ALU.mult).then_inc(
                *V.step("hidden", L, j))
            loop_low(k, dve, c0, 3 * j + 4, i)
            dve.wait_ge(*k.after("hidden hi", L, j, i=i))
            dve.tensor_tensor(k.HTL[:, :, :].rearrange("p a b -> p (a b)"), k.PS[:, 3, 0:DE],
                              k.HTH[:, :, :].rearrange("p a b -> p (a b)").bitcast(F32), ALU.subtract).then_inc(
                *V.step("hidden lo", L, j))
            loop_low(k, dve, c0, 3 * j + 5, i)
            dve.wait_ge(*k.after("down", L, j, i=i))
            dve.wait_ge(*k.after("scattered", L, (j - 2) % BODY, i=i, lag=0 if j >= 2 else 1))
            dve.tensor_copy(k.YB[:, j % 2, HALF:D], k.PS[:, 5, :]).then_inc(*V.step("moe y", L, j, 1))
        V.leave(NBLK // BODY)
    k.low_next = c0 + 3 * NBLK + MOE_LOOK
    if c0 + 3 * NBLK in k.UNUSED:
        for q in range(MOE_LOOK):
            V.mark("used", k.SPLIT_NO[c0 + 3 * NBLK + q])
    for q in range(MOE_LOOK):
        V.mark("low", c0 + 3 * NBLK + q)
        V.mark("raw free", c0 + 3 * NBLK + q)


def moe_gpsimd(k, pool, L, c0):
    xg = [k.counter(f"gathered{s}") for s in range(2)]
    ys = [k.counter(f"scattered{s}") for s in range(2)]
    G = k.G

    def index(slot, col):
        pool.wait_ge(*k.after("table read", L))
        pool.tensor_copy(k.IDX[:, slot:slot + 1], k.TAB[:, bass.ds(col, 1)]).then_inc(*G.step())
        pool.wait_ge(*G.now())
        pool.sem_inc(k.counter("index_seen").sem)

    def gather(b, j, *label):
        s = j % 2
        if xg[s].n:
            pool.wait_ge(*xg[s].now())
        index(s, 2 * b)
        pool.indirect_dma_start(k.XG[:, s, :], None, k.xn_d[:, :],
                                bass.IndirectOffsetOnAxis(ap=k.IDX[:, s:s + 1], axis=0)).then_inc(
            *xg[s].step(*label, by=16))
    if L == 0:
        for n, p in enumerate(xg[1:] + ys):
            pool.dma_start(k.PRIME[:, n, :], k.dram["const"][:, 0:8]).then_inc(*p.step(by=16))
    gather(0, 0, "first gathered", L)
    gather(1, 1, "second gathered", L)
    for half in range(2):
        pool.wait_ge(*k.after("first turned", L, half))
    with pool.Fori(0, NBLK // BODY) as i:
        for p in xg + ys + [G]:
            p.enter(i)
        for j in range(BODY):
            pool.wait_ge(*k.after("moe turned", L, j, 1, i=i, lag=0 if j else 1))
            gather(i * BODY + (j + 2), j + 2, "gathered", L, (j + 2) % BODY)
            for half in range(2):
                pool.wait_ge(*k.after("moe y", L, j, half, i=i))
            s = j % 2
            pool.wait_ge(*ys[s].now())
            index(2 + s, 2 * (i * BODY + j) + 1)
            pool.indirect_dma_start(k.y_d[:, :], bass.IndirectOffsetOnAxis(ap=k.IDX[:, 2 + s:3 + s], axis=0),
                                    k.YB[:, s, :], None, bounds_check=2 * (XT + 1) * P - 1, oob_is_err=False).then_inc(
                *ys[s].step("scattered", L, j, by=16))
        for p in xg + ys + [G]:
            p.leave(NBLK // BODY)
    for p in xg + ys:
        pool.wait_ge(*p.now())


def combine_gpsimd(k, sync, L, T):
    for t in range(T):
        n = tile_col(t)[1]
        if t >= 2:
            sync.wait_ge(*k.after("combined", L, t - 2))
        sync.dma_start(k.YC[0:n, t % 2, :], k.y_d[2 * P * t:2 * P * t + 2 * n, :].rearrange("(p c) d -> p (c d)", c=2)).then_inc(
            *k.counter(f"rows{t % 2}_loaded").step("rows", L, t, by=16))


def combine_vector(k, dve, L, T):
    for t in range(T):
        n = tile_col(t)[1]
        dve.wait_ge(*k.after("rows", L, t))
        for c in range(2):
            dve.wait_ge(*k.V.now())
            dve.scalar_tensor_tensor(out=k.H[0:n, t, :], in0=k.YC[0:n, t % 2, c * D:(c + 1) * D],
                                     scalar=k.GATE[0:n, c, t:t + 1], in1=k.H[0:n, t, :],
                                     op0=ALU.mult, op1=ALU.add).then_inc(*k.V.step("combined", L, t))



def high(k, act, dst, src, *label):
    act.activation(dst, src, ACT.Copy).then_inc(*k.A.step(*label))


def low(k, dve, dst, src, hi, *label):
    dve.tensor_tensor(dst, src, hi.bitcast(F32), ALU.subtract).then_inc(*k.V.step(*label))



CWID = KVR + ROPE
KHALF = KEYS // 2


def rotate(k, dve, dst, src, cos, sin, ta, tb):
    h = ROPE // 2
    n = len(src.shape)
    a, b = (src[:, :, 0:h], src[:, :, h:ROPE])
    da, db = (dst[:, :, 0:h], dst[:, :, h:ROPE])
    dve.wait_ge(*k.V.now())
    dve.tensor_tensor(ta, a, cos, ALU.mult).then_inc(*k.V.step())
    dve.tensor_tensor(tb, b, sin, ALU.mult).then_inc(*k.V.step())
    dve.wait_ge(*k.V.now())
    dve.tensor_tensor(da, ta, tb, ALU.subtract).then_inc(*k.V.step())
    dve.wait_ge(*k.V.now())
    dve.tensor_tensor(ta, a, sin, ALU.mult).then_inc(*k.V.step())
    dve.tensor_tensor(tb, b, cos, ALU.mult).then_inc(*k.V.step())
    dve.wait_ge(*k.V.now())
    dve.tensor_tensor(db, ta, tb, ALU.add).then_inc(*k.V.step())


def table3(k, name, t0, nt):
    at, _ = _C[name]
    h = ROPE // 2
    return k.CONST[:, at + t0 * h:at + (t0 + nt) * h].rearrange("p (t f) -> p t f", t=nt)


def latent_tensor(k, pe, *_):
    c = k.FIRST[("latent",)]
    norm_tensor(k, pe, "latent", range(XT + 1))
    for t in range(XT + 1):
        c0, n = tile_col(t)
        for half in range(2):
            pe.wait_ge(*k.after("latent", "out", t, half))
        if t == 4:
            pe.wait_ge(*k.after("c copied", 0))
        for q in range(2):
            wh, wl = chunk_pair(k, pe, c + q)
            for f in range(4):
                w = slice(f * CWID, f * CWID + CWID)
                mm = products(pe, k.PS[0:n, 4 + t % 4, 0:CWID], k.XH[:, 4 * q + f, c0:c0 + n], k.XL[:, 4 * q + f, c0:c0 + n],
                              wh[:, w], wl[:, w], q == 0 and f == 0, q == 1 and f == 3)
        mm.then_inc(*k.T.step("c", t))
    k.T.mark("used", k.SPLIT_NO[c])
    k.T.mark("used", k.SPLIT_NO[c + 1])
    pe.wait_ge(*k.after("c normed"))
    pe.wait_ge(*k.after("k turned by position"))
    for t in range(XT + 1):
        n = tile_col(t)[1]
        b = t % 4
        if t == 4:
            pe.wait_ge(*k.after("ck lo", 0))
            pe.wait_ge(*k.after("kr", 0))
        for f in range(2):
            pe.transpose(k.PS[:, b, f * P:f * P + n], k.CN[0:n, t, f * P:(f + 1) * P], k.CONST[0:n, 0:n])
        pe.transpose(k.PS[:, b, 2 * P:2 * P + n], k.KRD[0:n, t, :], k.CONST[0:n, 0:n]).then_inc(*k.T.step("ck turned", t))
    wh, wl = chunk_pair(k, pe, c + 2)
    pe.wait_ge(*k.after("ck lo", XT))
    pe.wait_ge(*k.after("kr", XT))
    r = 0
    for h in range(HEADS):
        for s in range(2):
            if r >= 8:
                pe.wait_ge(*k.after("kv out", r - 8))
            cols = slice(s * KHALF, s * KHALF + KHALF)
            for f in range(2):
                w = slice((2 * h + f) * P, (2 * h + f + 1) * P)
                mm = products(pe, k.PS[:, r % 8, 0:KHALF], wh[:, w], wl[:, w], k.CKH[:, f, cols], k.CKL[:, f, cols],
                              f == 0, f == 1)
            mm.then_inc(*k.T.step("kv", r))
            r += 1
    k.T.mark("used", k.SPLIT_NO[c + 2])
    wh, wl = chunk_pair(k, pe, c + 3)
    for t in range(XT + 1):
        c0, n = tile_col(t)
        for half in range(2):
            pe.wait_ge(*k.after("kv out", r - 8))
            for f in range(2):
                w = slice(f * D + half * HALF, f * D + half * HALF + HALF)
                mm = products(pe, k.PS[0:n, r % 8, :], k.CKH[:, f, c0:c0 + n], k.CKL[:, f, c0:c0 + n], wh[:, w], wl[:, w],
                              f == 0, f == 1)
            mm.then_inc(*k.T.step("kv", r))
            r += 1
    k.T.mark("used", k.SPLIT_NO[c + 3])


def kv_place(k, r):
    if r < 2 * HEADS:
        h, s = divmod(r, 2)
        return k.KT[:, h, s * KHALF:(s + 1) * KHALF], k.PS[:, r % 8, 0:KHALF]
    t, half = divmod(r - 2 * HEADS, 2)
    if t < XT:
        return k.VAL[:, t, half * HALF:(half + 1) * HALF], k.PS[:, r % 8, :]
    return k.H[0:META, XT, half * HALF:(half + 1) * HALF], k.PS[0:META, r % 8, :]


def latent_scalar(k, act, *_):
    c = k.FIRST[("latent",)]
    norm_scalar(k, act, "latent", range(XT + 1), "pair")
    split_high(k, act, c + LOOK)
    act.wait_ge(*k.after("c blank"))
    for t in range(XT + 1):
        n = tile_col(t)[1]
        act.wait_ge(*k.after("c", t))
        act.activation(k.CB[0:n, t, :], k.PS[0:n, 4 + t % 4, 0:CWID], ACT.Copy).then_inc(*k.A.step("c copied", t))
    for t in range(XT + 1):
        act.wait_ge(*k.A.now())
        act.activation(k.CN[:, t, :], k.CB[:, t, 0:KVR], ACT.Square, accum_out=k.SS[:, t:t + 1]).then_inc(*k.A.step())
    act.wait_ge(*k.A.now())
    act.activation(k.RT[:, 0:XT + 1], k.SS[:, 0:XT + 1], ACT.Sqrt, scale=1.0 / KVR, bias=const(k, "eps")).then_inc(
        *k.A.step("c root"))
    split_high(k, act, c + 3)
    for t in range(XT + 1):
        c0, n = tile_col(t)
        act.wait_ge(*k.after("ck turned", t))
        src = k.PS[:, t % 4, 0:2 * P].rearrange("p (a c) -> p a c", a=2)[:, :, 0:n]
        high(k, act, k.CKH[:, :, c0:c0 + n], src, "ck hi", t)
        act.activation(k.KR[:, c0:c0 + n], k.PS[:, t % 4, 2 * P:2 * P + n], ACT.Copy).then_inc(*k.A.step("kr", t))
    for r in range(2 * HEADS + 2 * (XT + 1)):
        if r == 2 * HEADS:
            split_high(k, act, c + 3 + LOOK)
        if r % 2 == 0:
            dst, src = kv_place(k, r)
            act.wait_ge(*k.after("kv", r))
            act.activation(dst, src, ACT.Copy).then_inc(*k.A.step("kv out", r))


def latent_vector(k, dve, *_):
    c = k.FIRST[("latent",)]
    norm_vector(k, dve, "latent", range(XT + 1), "pair", "kv_norm")
    split_low(k, dve, c + LOOK)
    for t in range(XT + 1):
        dve.wait_ge(*k.after("latent", "turned", t, 1))
    dve.memset(k.CB[:, XT, :], 0.0).then_inc(*k.V.step("c blank"))
    dve.wait_ge(*k.after("c root"))
    dve.wait_ge(*k.V.now())
    dve.reciprocal(k.RS[:, 0:XT + 1], k.RT[:, 0:XT + 1]).then_inc(*k.V.step())
    dve.wait_ge(*k.V.now())
    for t in range(XT + 1):
        dve.scalar_tensor_tensor(out=k.CN[:, t, :], in0=k.CB[:, t, 0:KVR], scalar=k.RS[:, t:t + 1], in1=param(k, "kvrow"),
                                 op0=ALU.mult, op1=ALU.mult).then_inc(*k.V.step("c normed"))
    rotate(k, dve, k.KRD[:, :, 0:ROPE], k.CB[:, :, KVR:CWID], table3(k, "cos", 0, XT + 1), table3(k, "sin", 0, XT + 1),
           k.TRA[:, :, :], k.TRB[:, :, :])
    dve.wait_ge(*k.V.now())
    dve.tensor_copy(k.KRD[:, :, ROPE:P], k.KRD[:, :, 0:ROPE]).then_inc(*k.V.step("k turned by position"))
    split_low(k, dve, c + 3)
    for t in range(XT + 1):
        c0, n = tile_col(t)
        dve.wait_ge(*k.after("kr", t))
        src = k.PS[:, t % 4, 0:2 * P].rearrange("p (a c) -> p a c", a=2)[:, :, 0:n]
        low(k, dve, k.CKL[:, :, c0:c0 + n], src, k.CKH[:, :, c0:c0 + n], "ck lo", t)
    for r in range(2 * HEADS + 2 * (XT + 1)):
        if r == 2 * HEADS:
            split_low(k, dve, c + 3 + LOOK)
        if r % 2:
            dst, src = kv_place(k, r)
            dve.wait_ge(*k.after("kv", r))
            dve.tensor_copy(dst, src).then_inc(*k.V.step("kv out", r))



def query_tensor(k, pe, *_):
    c = k.FIRST[("query",)]
    norm_tensor(k, pe, "query", range(XT))
    for t in range(XT):
        for half in range(2):
            pe.wait_ge(*k.after("query", "out", t, half))
        for q in range(2):
            wh, wl = chunk_pair(k, pe, c + q)
            for f in range(4):
                w = slice(f * QR, f * QR + QR)
                mm = products(pe, k.PS[:, 4 + t, 0:QR], k.XH[:, 4 * q + f, t * P:(t + 1) * P], k.XL[:, 4 * q + f, t * P:(t + 1) * P],
                              wh[:, w], wl[:, w], q == 0 and f == 0, q == 1 and f == 3)
        mm.then_inc(*k.T.step("cq", t))
    k.T.mark("used", k.SPLIT_NO[c])
    k.T.mark("used", k.SPLIT_NO[c + 1])
    for t in range(XT):
        pe.wait_ge(*k.after("cq normed", t))
        for f in range(3):
            mm = pe.transpose(k.PS[:, t, f * P:(f + 1) * P], k.CQN[:, t, f * P:(f + 1) * P], const(k, "ident"))
        mm.then_inc(*k.T.step("cq turned", t))
    wh, wl = chunk_pair(k, pe, c + 2)
    for t in range(XT):
        pe.wait_ge(*k.after("cq lo", t))
        for f in range(3):
            w = slice(f * HALF, f * HALF + HALF)
            mm = products(pe, k.PS[:, 4 + t, :], k.CQH[:, f, t * P:(t + 1) * P], k.CQL[:, f, t * P:(t + 1) * P],
                          wh[:, w], wl[:, w], f == 0, f == 2)
        mm.then_inc(*k.T.step("qr", t))
    k.T.mark("used", k.SPLIT_NO[c + 2])
    for t in range(XT):
        pe.wait_ge(*k.after("qr rotated", t))
        for f in range(4):
            mm = pe.transpose(k.PS[:, t, f * P:(f + 1) * P], k.QRB[:, t % 2, f * P:(f + 1) * P], const(k, "ident"))
        mm.then_inc(*k.T.step("qr turned", t))
    for h in range(HEADS):
        wh, wl = chunk_pair(k, pe, c + 3 + h // 4)
        if h >= 4:
            pe.wait_ge(*k.after("qn out", h - 4))
        else:
            pe.wait_ge(*k.after("qr rotated", h))
        for f in range(3):
            w = slice(((h % 4) * 3 + f) * P, ((h % 4) * 3 + f + 1) * P)
            mm = products(pe, k.PS[:, 4 + h % 4, :], wh[:, w], wl[:, w], k.CQH[:, f, :], k.CQL[:, f, :], f == 0, f == 2)
        mm.then_inc(*k.T.step("qn", h))
        if h % 4 == 3:
            k.T.mark("used", k.SPLIT_NO[c + 3 + h // 4])


def query_scalar(k, act, *_):
    c = k.FIRST[("query",)]
    norm_scalar(k, act, "query", range(XT), "pair")
    split_high(k, act, c + LOOK)
    for t in range(XT):
        act.wait_ge(*k.after("cq", t))
        act.wait_ge(*k.A.now())
        act.activation(k.SQ[:, 0:QR], k.PS[:, 4 + t, 0:QR], ACT.Square, accum_out=k.SS[:, t:t + 1]).then_inc(*k.A.step())
    act.wait_ge(*k.A.now())
    act.activation(k.RT[:, 0:XT], k.SS[:, 0:XT], ACT.Sqrt, scale=1.0 / QR, bias=const(k, "eps")).then_inc(*k.A.step("cq root"))
    split_high(k, act, c + 3)
    for t in range(XT):
        act.wait_ge(*k.after("cq turned", t))
        high(k, act, k.CQH[:, :, t * P:(t + 1) * P], k.PS[:, t, 0:QR].rearrange("p (a c) -> p a c", a=3), "cq hi", t)
    for t in range(XT):
        act.wait_ge(*k.after("qr turned", t))
        act.activation(k.QRT[:, :, t * P:(t + 1) * P], k.PS[:, t, :].rearrange("p (a c) -> p a c", a=4), ACT.Copy).then_inc(
            *k.A.step("qr out", t))
    split_high(k, act, c + 4)
    for h in range(HEADS):
        if h == 4:
            split_high(k, act, c + 4 + LOOK)
        act.wait_ge(*k.after("qn", h))
        act.activation(k.QN[:, h, :], k.PS[:, 4 + h % 4, :], ACT.Copy).then_inc(*k.A.step("qn out", h))


def query_vector(k, dve, *_):
    c = k.FIRST[("query",)]
    norm_vector(k, dve, "query", range(XT), "pair", "b_norm")
    split_low(k, dve, c + LOOK)
    dve.wait_ge(*k.after("cq root"))
    dve.wait_ge(*k.V.now())
    dve.reciprocal(k.RS[:, 0:XT], k.RT[:, 0:XT]).then_inc(*k.V.step())
    dve.wait_ge(*k.V.now())
    for t in range(XT):
        dve.scalar_tensor_tensor(out=k.CQN[:, t, :], in0=k.PS[:, 4 + t, 0:QR], scalar=k.RS[:, t:t + 1], in1=param(k, "qrow"),
                                 op0=ALU.mult, op1=ALU.mult).then_inc(*k.V.step("cq normed", t))
    split_low(k, dve, c + 3)
    for t in range(XT):
        dve.wait_ge(*k.after("cq hi", t))
        cols = slice(t * P, (t + 1) * P)
        low(k, dve, k.CQL[:, :, cols], k.PS[:, t, 0:QR].rearrange("p (a c) -> p a c", a=3), k.CQH[:, :, cols], "cq lo", t)
    for t in range(XT):
        dve.wait_ge(*k.after("qr", t))
        if t >= 2:
            dve.wait_ge(*k.after("qr turned", t - 2))
        bc = [table3(k, n, t, 1).to_broadcast([P, HEADS, ROPE // 2]) for n in ("cos", "sin")]
        rotate(k, dve, k.QRB[:, t % 2, :].rearrange("p (h f) -> p h f", h=HEADS),
               k.PS[:, 4 + t, :].rearrange("p (h f) -> p h f", h=HEADS), *bc, k.TQA[:, :, :], k.TQB[:, :, :])
        k.V.mark("qr rotated", t)
    split_low(k, dve, c + 4)
    split_low_at = c + 4 + LOOK
    dve.wait_ge(*k.after("qn", 3))
    split_low(k, dve, split_low_at)



def mla_span(u):
    h, i = divmod(u, XT)
    a = (2 * (u % 2)) * HALF + HALF - P * (i + 1)
    return h, i, a, P * (i + 1) + META


UNITS = HEADS * XT


def attend_tensor(k, pe, *_):
    def scores(u):
        h, i, a, n = mla_span(u)
        if u >= 2:
            pe.wait_ge(*k.after("prob", u - 2))
        q, keys = slice(i * P, (i + 1) * P), slice(0, (i + 1) * P)
        r = slice(64 * (h % 2), 64 * (h % 2) + 64)
        out = flat(k, a, a + n - META)
        pe.matmul(out, k.QN[:, h, q], k.KT[:, h, keys], start=True, stop=False)
        pe.matmul(out, k.QRT[r, h // 2, q], k.KR[r, keys], start=False, stop=False)
        pe.matmul(flat(k, a + n - META - P, a + n - META), const(k, "ident"), const(k, "future"), start=False, stop=True)
        out = flat(k, a + n - META, a + n)
        pe.matmul(out, k.QN[:, h, q], k.KT[:, h, SEQ:KEYS], start=True, stop=False)
        pe.matmul(out, k.QRT[r, h // 2, q], k.KR[r, SEQ:KEYS], start=False, stop=True).then_inc(*k.T.step("scores", u))

    def turn(u):
        h, i, a, n = mla_span(u)
        pe.wait_ge(*k.after("prob normed", u))
        if u >= 1:
            pe.wait_ge(*k.after("pt", u - 1))
            pe.wait_ge(*k.after("pt meta", u - 1))
        for j in range(i + 1):
            pe.transpose(flat(k, (4 + 0) * HALF + j * P, 4 * HALF + (j + 1) * P), k.PR[u % 2][:, j * P:(j + 1) * P], const(k, "ident"))
        pe.transpose(k.PS[0:META, 5, 0:P], k.PR[u % 2][:, n - META:n], const(k, "ident")).then_inc(*k.T.step("prob turned", u))

    def values(u):
        h, i, a, n = mla_span(u)
        pe.wait_ge(*k.after("pt", u))
        pe.wait_ge(*k.after("pt meta", u))
        if u >= 2:
            pe.wait_ge(*k.after("o lo", u - 2))
        v = slice(h * VD, (h + 1) * VD)
        out = k.PS[:, 6 + u % 2, 0:P]
        for j in range(i + 1):
            pe.matmul(out, k.VAL[:, j, v], k.PT[u % 2][:, j, :], start=(j == 0), stop=False)
        pe.matmul(out, k.H[0:META, XT, v], k.PT[u % 2][0:META, XT - 1 + u % 2, :], start=False, stop=True).then_inc(*k.T.step("o", u))
    scores(0)
    scores(1)
    for u in range(UNITS):
        turn(u)
        if u + 2 < UNITS:
            scores(u + 2)
        if u >= 1:
            values(u - 1)
    values(UNITS - 1)


def attend_scalar(k, act, *_):
    def prob(u):
        h, i, a, n = mla_span(u)
        act.wait_ge(*k.after("top", u))
        if u >= 2:
            act.wait_ge(*k.after("prob turned", u - 2))
        act.activation(k.PR[u % 2][:, 0:n], flat(k, a, a + n), ACT.Exp, scale=MLA_SCALE, bias=k.TOP[:, 2 + u % 2:3 + u % 2],
                       accum_out=k.SUM[:, u % 2:u % 2 + 1]).then_inc(*k.A.step("prob", u))
    def o_high(u):
        h, i, a, n = mla_span(u)
        act.wait_ge(*k.after("o", u))
        high(k, act, k.OTH[:, h, i * P:(i + 1) * P], k.PS[:, 6 + u % 2, 0:P], "o hi", u)
    prob(0)
    for u in range(UNITS):
        h, i, a, n = mla_span(u)
        if u + 1 < UNITS:
            prob(u + 1)
        act.wait_ge(*k.after("prob turned", u))
        if u >= 2:
            act.wait_ge(*k.after("o", u - 2))
        act.activation(k.PT[u % 2][:, 0:i + 1, :].rearrange("p a b -> p (a b)"), flat(k, 4 * HALF, 4 * HALF + (i + 1) * P),
                       ACT.Copy).then_inc(*k.A.step("pt", u))
        if u >= 1:
            o_high(u - 1)
    o_high(UNITS - 1)


def attend_vector(k, dve, *_):
    V = k.V

    def top(u):
        h, i, a, n = mla_span(u)
        dve.wait_ge(*k.after("scores", u))
        if u >= 2:
            dve.wait_ge(*k.after("prob", u - 2))
        dve.wait_ge(*V.now())
        dve.tensor_reduce(k.TOP[:, u % 2:u % 2 + 1], flat(k, a, a + n), AX.X, ALU.max).then_inc(*V.step())
        dve.wait_ge(*V.now())
        dve.tensor_scalar(k.TOP[:, 2 + u % 2:3 + u % 2], k.TOP[:, u % 2:u % 2 + 1], -MLA_SCALE, None, ALU.mult).then_inc(
            *V.step("top", u))
    def normed(u):
        h, i, a, n = mla_span(u)
        dve.wait_ge(*k.after("prob", u))
        dve.wait_ge(*V.now())
        dve.reciprocal(k.TOP[:, 4 + u % 2:5 + u % 2], k.SUM[:, u % 2:u % 2 + 1]).then_inc(*V.step())
        dve.wait_ge(*V.now())
        dve.tensor_scalar(k.PR[u % 2][:, 0:n], k.PR[u % 2][:, 0:n], k.TOP[:, 4 + u % 2:5 + u % 2], None, ALU.mult).then_inc(
            *V.step("prob normed", u))

    def o_low(u):
        h, i, a, n = mla_span(u)
        dve.wait_ge(*k.after("o hi", u))
        low(k, dve, k.OTL[:, h, i * P:(i + 1) * P], k.PS[:, 6 + u % 2, 0:P], k.OTH[:, h, i * P:(i + 1) * P], "o lo", u)
    top(0)
    normed(0)
    top(1)
    for u in range(UNITS):
        if u + 1 < UNITS:
            normed(u + 1)
        dve.wait_ge(*k.after("prob turned", u))
        if u >= 2:
            dve.wait_ge(*k.after("o", u - 2))
        dve.tensor_copy(k.PT[u % 2][0:META, XT - 1 + u % 2, :], k.PS[0:META, 5, 0:P]).then_inc(*V.step("pt meta", u))
        if u + 2 < UNITS:
            top(u + 2)
        if u >= 1:
            o_low(u - 1)
    o_low(UNITS - 1)



def rows_tensor(k, pe, name, c, ah, al):
    for half in range(2):
        for q in range(2):
            wh, wl = chunk_pair(k, pe, c + 2 * half + q)
            for t in range(XT):
                for f in range(4):
                    w = slice(f * HALF, f * HALF + HALF)
                    mm = products(pe, k.PS[:, 4 * half + t, :], ah[:, 4 * q + f, t * P:(t + 1) * P],
                                  al[:, 4 * q + f, t * P:(t + 1) * P], wh[:, w], wl[:, w],
                                  q == 0 and f == 0, q == 1 and f == 3)
                if q == 1 and t < XT - 1:
                    mm.then_inc(*k.T.step(name, half, t))
            mm.then_inc(*k.T.step("used", k.SPLIT_NO[c + 2 * half + q]))
            if q == 1:
                k.T.mark(name, half, XT - 1)


def attout_tensor(k, pe):
    rows_tensor(k, pe, "att rows", k.FIRST[("attout",)], k.OTH, k.OTL)


def attout_scalar(k, act):
    split_high(k, act, k.FIRST[("attout",)] + 3)


def attout_vector(k, dve):
    split_low(k, dve, k.FIRST[("attout",)] + 3)
    for half in range(2):
        for t in range(XT):
            dve.wait_ge(*k.after("att rows", half, t))
            cols = slice(half * HALF, half * HALF + HALF)
            dve.tensor_tensor(k.H[:, t, cols], k.H[:, t, cols], k.PS[:, 4 * half + t, :], ALU.add).then_inc(*k.V.step())



def last_scalar(k, act):
    norm_scalar(k, act, "last", range(XT), None)


def last_vector(k, dve):
    dve.wait_ge(*k.after("last", "root"))
    dve.reciprocal(k.RS[:, 0:XT], k.RT[:, 0:XT]).then_inc(*k.V.step())
    dve.wait_ge(*k.V.now())
    dve.wait_ge(*k.after("row", "final"))
    for t in range(XT):
        dve.scalar_tensor_tensor(out=k.H[:, t, :], in0=k.H[:, t, :], scalar=k.RS[:, t:t + 1], in1=row(k, "final"),
                                 op0=ALU.mult, op1=ALU.mult).then_inc(*k.V.step())
    k.V.mark("row done", "final")



ADAW = 3 * D // 2


def ada_scalar(k, act, s):
    if s == 0:
        split_high(k, act, k.FIRST[("ada", 0)] - 1)
        act.activation(k.CS[:, :], param(k, "c"), ACT.Silu).then_inc(*k.A.step("condition"))
    for f in range(DK):
        act.wait_ge(*k.after("u", s, f))
        if f == 0 and s == 0:
            pass
        high(k, act, k.XH[:, f, 0:SEQ], k.UT[:, f % 2, :], "u hi", s, f)


def ada_vector(k, dve, s):
    c = k.FIRST[("ada", s)]
    if s == 0:
        split_low(k, dve, c - 1)
    dve.wait_ge(*k.after("condition"))
    for q in range(2 * DK):
        f, half = divmod(q, 2)
        acc = k.ACC[:, half * ADAW:(half + 1) * ADAW]
        w = k.RAW[(c + q) % RAW_SLOTS][:, 0:ADAW]
        dve.wait_ge(*k.after("raw", c + q))
        if f == 0:
            dve.tensor_scalar(acc, w, k.CS[:, f:f + 1], None, ALU.mult).then_inc(*k.V.step("raw free", c + q))
        else:
            dve.wait_ge(*k.V.now())
            dve.scalar_tensor_tensor(out=acc, in0=w, scalar=k.CS[:, f:f + 1], in1=acc, op0=ALU.mult, op1=ALU.add).then_inc(
                *k.V.step("raw free", c + q))
    k.V.mark("acc", s)
    k.low_next = c + 2 * DK
    k.high_next = max(k.high_next, c + 2 * DK)
    dve.wait_ge(*k.after("sums", s))
    at, _ = _R["adab"]
    at += 16 * s
    dve.tensor_tensor(k.SHC[:, :], k.PS[:, 0, 0:DK], k.PARAM[:, at:at + DK], ALU.add).then_inc(*k.V.step())
    dve.scalar_tensor_tensor(out=k.SCC[:, :], in0=k.PS[:, 0, DK:2 * DK], scalar=1.0, in1=k.PARAM[:, at + DK:at + 2 * DK],
                             op0=ALU.add, op1=ALU.add).then_inc(*k.V.step())
    g = row(k, f"gate{s}")
    dve.wait_ge(*k.after("row", f"gate{s}"))
    dve.scalar_tensor_tensor(out=g, in0=flat(k, 2 * HALF, 4 * HALF), scalar=1.0, in1=g, op0=ALU.add, op1=ALU.add).then_inc(
        *k.V.step())
    dve.wait_ge(*k.V.now())
    for f in range(DK):
        def u(f):
            dve.wait_ge(*k.after("x turned", s, f))
            if f >= 2:
                dve.wait_ge(*k.after("u lo", s, f - 2))
            dve.tensor_scalar(k.UT[:, f % 2, :], k.PS[:, 4 + f % 4, :], k.SCC[:, f:f + 1], k.SHC[:, f:f + 1],
                              ALU.mult, ALU.add).then_inc(*k.V.step("u", s, f))
        if f == 0:
            u(0)
        if f + 1 < DK:
            if f >= 1:
                dve.wait_ge(*k.after("u hi", s, f - 1))
            u(f + 1)
        dve.wait_ge(*k.after("u hi", s, f))
        low(k, dve, k.XL[:, f, 0:SEQ], k.UT[:, f % 2, :], k.XH[:, f, 0:SEQ], "u lo", s, f)


def ada_tensor(k, pe, s):
    for f in range(4):
        turn_x(k, pe, s, f)
    pe.wait_ge(*k.after("acc", s))
    for m in range(2 * DK):
        pe.matmul(k.PS[:, 0, m:m + 1], k.ACC[:, m * P:(m + 1) * P], const(k, "ones")[:, 0:1], start=True, stop=True)
    for half in range(2):
        mm = pe.matmul(k.PS[:, 2 + half, :], const(k, "ones"), k.ACC[:, 2 * D + half * HALF:2 * D + (half + 1) * HALF],
                       start=True, stop=True)
    mm.then_inc(*k.T.step("sums", s))
    for f in range(4, DK):
        turn_x(k, pe, s, f)


def turn_x(k, pe, s, f):
    if f >= 4:
        pe.wait_ge(*k.after("u", s, f - 4))
    for t in range(XT):
        mm = pe.transpose(k.PS[:, 4 + f % 4, t * P:(t + 1) * P], k.H[:, t, f * P:(f + 1) * P], const(k, "ident"))
    mm.then_inc(*k.T.step("x turned", s, f))



def residual(k, dve, half, t, y, s, n):
    cols = slice(half * HALF, half * HALF + HALF)
    tmp = k.RESID[:, n % 2, :]
    dve.wait_ge(*k.V.now())
    dve.tensor_tensor(tmp, y, row(k, f"gate{s}")[:, cols], ALU.mult).then_inc(*k.V.step())
    dve.wait_ge(*k.V.now())
    dve.scalar_tensor_tensor(out=k.H[:, t, cols], in0=k.H[:, t, cols], scalar=ALPHA, in1=tmp,
                             op0=ALU.mult, op1=ALU.add).then_inc(*k.V.step())


def layernorm_vector(k, dve, s):
    V = k.V
    k.V.mark("row done", f"gate{s}")
    for t in range(XT):
        for half in range(2):
            dve.bn_stats(k.BN[:, t, 6 * half:6 * half + 6], k.H[:, t, half * HALF:(half + 1) * HALF]).then_inc(*V.step())
    dve.wait_ge(*V.now())
    for t in range(XT):
        dve.bn_aggr(k.MV[:, t, :], k.BN[:, t, :]).then_inc(*V.step())
    V.mark("moments", s)
    dve.wait_ge(*k.after("ln root", s))
    dve.reciprocal(k.RS[:, 0:XT], k.RT[:, 0:XT]).then_inc(*V.step())
    dve.wait_ge(*V.now())
    dve.wait_ge(*k.after("row", f"lng{s}"))
    dve.wait_ge(*k.after("row", f"lnb{s}"))
    for t in range(XT):
        dve.tensor_scalar(k.H[:, t, :], k.H[:, t, :], k.MV[:, t, 0:1], k.RS[:, t:t + 1], ALU.subtract, ALU.mult).then_inc(*V.step())
        dve.wait_ge(*V.now())
        dve.tensor_tensor(k.H[:, t, :], k.H[:, t, :], row(k, f"lng{s}"), ALU.mult).then_inc(*V.step())
        dve.wait_ge(*V.now())
        dve.tensor_tensor(k.H[:, t, :], k.H[:, t, :], row(k, f"lnb{s}"), ALU.add).then_inc(*V.step())
    V.mark("row done", f"lng{s}")
    V.mark("row done", f"lnb{s}")


def layernorm_scalar(k, act, s):
    act.wait_ge(*k.after("moments", s))
    act.activation(k.RT[:, 0:XT], k.MV[:, :, 1:2].rearrange("p t o -> p (t o)"), ACT.Sqrt, bias=const(k, "lneps")).then_inc(
        *k.A.step("ln root", s))



EVT = 16
RGT = 4


def even_in_tensor(k, pe):
    c = k.FIRST[("even_in",)]
    for m in range(EVT):
        wh, wl = chunk_pair(k, pe, c + m // 2)
        if m >= 4:
            pe.wait_ge(*k.after("ev out", m - 4))
        for f in range(DK):
            w = slice(((m % 2) * DK + f) * P, ((m % 2) * DK + f + 1) * P)
            mm = products(pe, k.PS[:, m % 4, :], wh[:, w], wl[:, w], k.XH[:, f, 0:SEQ], k.XL[:, f, 0:SEQ], f == 0, f == DK - 1)
        mm.then_inc(*k.T.step("ev", m))
        if m % 2:
            k.T.mark("used", k.SPLIT_NO[c + m // 2])
    for q in range(2):
        wh, wl = chunk_pair(k, pe, c + 8 + q)
        for t in range(XT):
            for f in range(4):
                w = slice(f * HALF, f * HALF + HALF)
                mm = products(pe, k.PS[:, 4 + t, :], k.XH[:, 4 * q + f, t * P:(t + 1) * P], k.XL[:, 4 * q + f, t * P:(t + 1) * P],
                              wh[:, w], wl[:, w], q == 0 and f == 0, q == 1 and f == 3)
        mm.then_inc(*k.T.step("used", k.SPLIT_NO[c + 8 + q]))
    k.T.mark("ev v")
    wh, wl = chunk_pair(k, pe, c + 10)
    pe.wait_ge(*k.after("ev out", EVT - 4))
    for f in range(DK):
        w = slice(f * 16, f * 16 + 16)
        mm = products(pe, k.PS[0:16, 0, :], wh[:, w], wl[:, w], k.XH[:, f, 0:SEQ], k.XL[:, f, 0:SEQ], f == 0, f == DK - 1)
    mm.then_inc(*k.T.step("used", k.SPLIT_NO[c + 10]))
    k.T.mark("ev z")


def even_in_scalar(k, act):
    c = k.FIRST[("even_in",)]
    split_high(k, act, c + LOOK)
    for m in range(EVT):
        act.wait_ge(*k.after("ev", m))
        if m % 2:
            split_high(k, act, c + m // 2 + LOOK)
        src = k.PS[:, m % 4, :]
        if m < 4:
            dst, f, scale = k.XR[:, m, 3:3 + SEQ], ACT.Copy, 1.0
        elif m < 8:
            dst, f, scale = k.YR[:, m - 4, :], ACT.Gelu_apprx_tanh, 1.0
        elif m < 10:
            dst, f, scale = k.GQ[:, m - 8, :], ACT.Copy, 0.125
        elif m < 12:
            dst, f, scale = k.GK[:, m - 10, :], ACT.Copy, 1.0
        else:
            dst, f, scale = k.GS[:, m - 12, :], ACT.Silu, 1.0
        act.activation(dst, src, f, scale=scale).then_inc(*k.A.step("ev out", m))
    split_high(k, act, c + 10)
    act.wait_ge(*k.after("ev v"))
    for t in range(XT):
        act.activation(k.GV[:, t, :], k.PS[:, 4 + t, :], ACT.Copy).then_inc(*k.A.step())
    act.wait_ge(*k.after("ev z"))
    act.activation(k.ZL[:, :], k.PS[0:16, 0, :], ACT.Copy).then_inc(*k.A.step())
    split_high(k, act, c + 10 + LOOK)


def even_in_vector(k, dve):
    c = k.FIRST[("even_in",)]
    dve.memset(k.XR[:, :, 0:3], 0.0).then_inc(*k.V.step())
    for n in range(2, 11 + LOOK):
        split_low(k, dve, c + n)



def log_sigmoid_vector(k, dve, x, e, z, q, *label):
    V = k.V

    def do(f, *a, **b):
        dve.wait_ge(*V.now())
        f(*a, **b).then_inc(*V.step())
    do(dve.scalar_tensor_tensor, out=e, in0=x, scalar=-1.0, in1=x, op0=ALU.mult, op1=ALU.max)
    V.mark(*label, "abs")
    do(dve.tensor_scalar, x, x, 0.0, None, ALU.min)
    dve.wait_ge(*k.after(*label, "exp"))
    do(dve.tensor_scalar, z, e, 2.0, None, ALU.add)
    do(dve.reciprocal, z, z)
    do(dve.tensor_tensor, z, z, e, ALU.mult)
    do(dve.tensor_tensor, q, z, z, ALU.mult)
    do(dve.tensor_scalar, e, q, 1.0 / 17, None, ALU.mult)
    for n in (15, 13, 11, 9, 7, 5, 3):
        do(dve.scalar_tensor_tensor, out=e, in0=e, scalar=1.0 / n, in1=q, op0=ALU.add, op1=ALU.mult)
    do(dve.scalar_tensor_tensor, out=e, in0=e, scalar=1.0, in1=z, op0=ALU.add, op1=ALU.mult)
    do(dve.scalar_tensor_tensor, out=x, in0=e, scalar=-2.0, in1=x, op0=ALU.mult, op1=ALU.add)


def log_sigmoid_scalar(k, act, e, *label):
    act.wait_ge(*k.after(*label, "abs"))
    act.activation(e, e, ACT.Exp, scale=-1.0).then_inc(*k.A.step(*label, "exp"))



def lru_gpsimd(k, pool):
    pool.dma_start(k.H[:, XT, :], k.dram["rg"]).then_inc(*k.counter("rg_loaded").step("rg", by=16))
    pool.dma_start(k.WUP[:, :], k.dram["wup"]).then_inc(*k.counter("wup_loaded").step("wup", by=16))


def lru_tensor(k, pe):
    pe.wait_ge(*k.after("rg"))
    for m in range(RGT):
        pe.wait_ge(*k.after("conv", m))
        if m >= 1:
            pe.wait_ge(*k.after("gates out", m - 1))
        for g in range(2):
            mm = pe.matmul(k.PS[:, 2 * (m % 2) + g, :], k.H[:, XT, (4 * g + m) * P:(4 * g + m + 1) * P], k.LT[:, 0, :],
                           start=True, stop=True)
        mm.then_inc(*k.T.step("gates", m))


def lru_scalar(k, act):
    A = k.A
    log_sigmoid_scalar(k, act, k.LM[:, 1, :], "lam")
    for m in range(RGT):
        act.wait_ge(*k.after("gates", m))
        if m >= 1:
            act.wait_ge(*k.after("mix lo", m - 1))
        else:
            act.wait_ge(*k.after("lam done"))
        act.activation(k.LT[:, 1, :], k.PS[:, 2 * (m % 2), :], ACT.Sigmoid, bias=param(k, "ba", m, 1)).then_inc(*A.step())
        act.activation(k.LT[:, 2, :], k.PS[:, 2 * (m % 2) + 1, :], ACT.Sigmoid, bias=param(k, "bx", m, 1)).then_inc(*A.step("gates out", m))
        act.wait_ge(*A.now())
        act.activation(k.LT[:, 3, :], k.LT[:, 1, :], ACT.Exp, scale=k.LM[:, 0, m:m + 1]).then_inc(*A.step())
        act.activation(k.LT[:, 4, :], k.LT[:, 1, :], ACT.Tanh, scale=k.LM[:, 4, m:m + 1]).then_inc(*A.step("decays", m))
        act.wait_ge(*k.after("inner", m))
        act.activation(k.LT[:, 4, :], k.LT[:, 4, :], ACT.Sqrt).then_inc(*A.step("rooted", m))
        act.wait_ge(*k.after("rg out", m))
        high(k, act, k.XH[:, m, 0:SEQ], k.LT[:, 0, :], "mix hi", m)


def lru_vector(k, dve):
    V = k.V

    def do(f, *a, **b):
        dve.wait_ge(*V.now())
        f(*a, **b).then_inc(*V.step())
    do(dve.tensor_copy, k.LM[:, 0, :], param(k, "lam"))
    log_sigmoid_vector(k, dve, k.LM[:, 0, :], k.LM[:, 1, :], k.LM[:, 2, :], k.LM[:, 3, :], "lam")
    do(dve.tensor_scalar, k.LM[:, 0, :], k.LM[:, 0, :], 8.0, None, ALU.mult)
    do(dve.tensor_scalar, k.LM[:, 4, :], k.LM[:, 0, :], -1.0, None, ALU.mult)
    V.mark("lam done")
    c, r, i, a, s = (k.LT[:, n, :] for n in range(5))
    for m in range(RGT):
        if m:
            dve.wait_ge(*k.after("mix hi", m - 1))
        do(dve.tensor_scalar, c, k.XR[:, m, 3:3 + SEQ], param(k, "convw", 12 + m, 1), param(k, "convb", m, 1), ALU.mult, ALU.add)
        for j in (2, 1, 0):
            do(dve.scalar_tensor_tensor, out=c, in0=k.XR[:, m, j:j + SEQ], scalar=param(k, "convw", 4 * j + m, 1), in1=c,
               op0=ALU.mult, op1=ALU.add)
        V.mark("conv", m)
        dve.wait_ge(*k.after("decays", m))
        do(dve.tensor_scalar, r, s, 1.0, None, ALU.add)
        do(dve.reciprocal, r, r)
        do(dve.scalar_tensor_tensor, out=s, in0=s, scalar=2.0, in1=r, op0=ALU.mult, op1=ALU.mult)
        V.mark("inner", m)
        do(dve.tensor_tensor, i, i, c, ALU.mult)
        dve.wait_ge(*k.after("rooted", m))
        do(dve.tensor_tensor, i, i, s, ALU.mult)
        do(dve.tensor_tensor_scan, r, a, i, 0.0, ALU.mult, ALU.add)
        do(dve.tensor_tensor, c, r, k.YR[:, m, :], ALU.mult)
        V.mark("rg out", m)
        dve.wait_ge(*k.after("mix hi", m))
        low(k, dve, k.XL[:, m, 0:SEQ], c, k.XH[:, m, 0:SEQ], "mix lo", m)



GCH = 64
NCH = SEQ // GCH
GH = 4
GLA_TAU = 16.0


def gla_tensor(k, pe):
    T = k.T
    pe.wait_ge(*k.after("wup"))
    for j in range(2):
        mm = pe.matmul(k.PS[:, j, :], k.WUP[:, j * P:(j + 1) * P], k.ZL[:, :], start=True, stop=True)
        mm.then_inc(*T.step("gate logits", j))
    for j in range(2):
        pe.wait_ge(*k.after("k end", j))
        for t in range(XT):
            mm = pe.transpose(k.PS[:, 2 + j, t * P:(t + 1) * P], k.GK[:, j, t * P:(t + 1) * P], const(k, "ident"))
        mm.then_inc(*T.step("k end turned", j))
    for j in range(2):
        pe.wait_ge(*k.after("k end out", j))
        for n in range(NCH - 1):
            if n >= 4:
                pe.wait_ge(*k.after("state", j, n - 4))
            elif j == 1:
                pe.wait_ge(*k.after("state", 0, NCH - 2))
            r = slice(GCH * (n % 2), GCH * (n % 2) + GCH)
            mm = pe.matmul(k.PS[:, 4 + n % 4, 0:2 * P], k.KET[r, j, n // 2, :],
                           k.GV[r, n // 2, 2 * j * P:(2 * j + 2) * P], start=True, stop=True)
            mm.then_inc(*T.step("kv chunk", j, n))
    for h in range(GH):
        j, p = divmod(h, 2)
        r = slice(64 * p, 64 * p + 64)
        pe.wait_ge(*k.after("q and k decayed"))
        if h >= 2:
            pe.wait_ge(*k.after("masked", h - 2))
        for t in range(XT):
            cols = slice(t * P, (t + 1) * P)
            mm = pe.matmul(k.PS[:, h % 2, cols], k.KD[r, j, cols], k.GQ[r, j, cols], start=True, stop=True)
        mm.then_inc(*T.step("gla scores", h))
        pe.wait_ge(*k.after("masked", h))
        pe.wait_ge(*k.after("states done"))
        if h >= 2:
            pe.wait_ge(*k.after("gla o read", h - 2))
        out = k.PS[:, 2 + h % 2, :]
        for t in range(XT):
            pe.matmul(out[:, t * P:(t + 1) * P], k.GV[:, t, h * P:(h + 1) * P], k.AT[:, h % 2, t * P:(t + 1) * P],
                      start=True, stop=False)
            for n in (2 * t, 2 * t + 1):
                cols = slice(n * GCH, (n + 1) * GCH)
                mm = pe.matmul(out[:, cols], k.ST[r, j, n, :], k.GQ[r, j, cols], start=False, stop=(n % 2 == 1))
        mm.then_inc(*T.step("gla o", h))
        pe.wait_ge(*k.after("gla squares", h))
        if h >= 2:
            pe.wait_ge(*k.after("gla root", h - 2))
        pe.matmul(k.PS[:, 4 + h % 2, :], const(k, "ones"), k.GT[:, h % 2, :], start=True, stop=True).then_inc(
            *T.step("gla sums", h))


def gla_scalar(k, act):
    A = k.A
    x, e, z, q = (k.LT[:, n, :] for n in range(4))
    for j in range(2):
        log_sigmoid_scalar(k, act, e, "gla", j)
        act.wait_ge(*k.after("bcum", j))
        act.activation(q, z, ACT.Exp).then_inc(*A.step("exp b", j))
        act.activation(e, z, ACT.Exp, scale=-1.0).then_inc(*A.step("exp -b", j))
        act.activation(k.DCY[:, j, :], z[:, GCH - 1:SEQ:GCH], ACT.Exp).then_inc(*A.step())
        act.wait_ge(*k.after("b end", j))
        act.activation(x, x, ACT.Exp).then_inc(*A.step("exp end", j))
    for j in range(2):
        act.wait_ge(*k.after("k end turned", j))
        act.activation(k.KET[:, j, :, :].rearrange("p a b -> p (a b)"), k.PS[:, 2 + j, :], ACT.Copy).then_inc(
            *A.step("k end out", j))
    for h in range(GH):
        act.wait_ge(*k.after("gla o", h))
        if h >= 2:
            act.wait_ge(*k.after("mix lo", h - 2 + 4))
        act.activation(k.GT[:, h % 2, :], k.PS[:, 2 + h % 2, :], ACT.Square).then_inc(*A.step("gla squares", h))
        act.wait_ge(*k.after("gla sums", h))
        act.activation(k.GT[:, h % 2, :], k.PS[:, 4 + h % 2, :], ACT.Sqrt, scale=1.0 / P, bias=const(k, "eps")).then_inc(
            *A.step("gla root", h))
        act.wait_ge(*k.after("gla out", h))
        high(k, act, k.XH[:, 4 + h, 0:SEQ], k.GT[:, h % 2, :], "mix hi", 4 + h)


def gla_vector(k, dve):
    V = k.V

    def do(f, *a, **b):
        dve.wait_ge(*V.now())
        f(*a, **b).then_inc(*V.step())
    x, e, z, q, tmp = (k.LT[:, n, :] for n in range(5))
    do(dve.memset, k.RESET[:, :], 1.0)
    do(dve.memset, k.RESET[:, 0:SEQ:GCH], 0.0)
    for j in range(2):
        dve.wait_ge(*k.after("gate logits", j))
        do(dve.tensor_scalar, x, k.PS[:, j, :], param(k, "bup", j, 1), None, ALU.add)
        log_sigmoid_vector(k, dve, x, e, z, q, "gla", j)
        do(dve.tensor_scalar, x, x, 1.0 / GLA_TAU, None, ALU.mult)
        do(dve.tensor_tensor_scan, z, k.RESET[:, :], x, 0.0, ALU.mult, ALU.add)
        V.mark("bcum", j)
        z3 = z.rearrange("p (n c) -> p n c", n=NCH)
        do(dve.tensor_tensor, x.rearrange("p (n c) -> p n c", n=NCH), z3[:, :, GCH - 1:GCH].to_broadcast([P, NCH, GCH]), z3,
           ALU.subtract)
        V.mark("b end", j)
        dve.wait_ge(*k.after("exp b", j))
        do(dve.tensor_tensor, k.GQ[:, j, :], k.GQ[:, j, :], q, ALU.mult)
        dve.wait_ge(*k.after("exp -b", j))
        do(dve.tensor_tensor, k.KD[:, j, :], k.GK[:, j, :], e, ALU.mult)
        V.mark("q and k decayed")
        dve.wait_ge(*k.after("exp end", j))
        do(dve.tensor_tensor, k.GK[:, j, :], k.GK[:, j, :], x, ALU.mult)
        V.mark("k end", j)
    do(dve.memset, k.ST[:, :, 0, :], 0.0)
    for j in range(2):
        for n in range(NCH - 1):
            dve.wait_ge(*k.after("kv chunk", j, n))
            dve.wait_ge(*V.now())
            for p in range(2):
                r = slice(64 * p, 64 * p + 64)
                dve.scalar_tensor_tensor(out=k.ST[r, j, n + 1, :], in0=k.ST[r, j, n, :], scalar=k.DCY[r, j, n:n + 1],
                                         in1=k.PS[r, 4 + n % 4, p * P:(p + 1) * P],
                                         op0=ALU.mult, op1=ALU.add).then_inc(*V.step("state", j, n))
    V.mark("states done")
    mask = const(k, "chunkmask").unsqueeze(1).to_broadcast([P, XT, P])
    for h in range(GH):
        dve.wait_ge(*k.after("gla scores", h))
        if h >= 2:
            dve.wait_ge(*k.after("gla o", h - 2))
        do(dve.tensor_tensor, k.AT[:, h % 2, :].rearrange("p (t c) -> p t c", t=XT),
           k.PS[:, h % 2, :].rearrange("p (t c) -> p t c", t=XT), mask, ALU.mult)
        V.mark("masked", h)
        dve.wait_ge(*k.after("gla root", h))
        g = k.GT[:, h % 2, :]
        do(dve.reciprocal, g, g)
        do(dve.tensor_tensor, g, k.PS[:, 2 + h % 2, :], g, ALU.mult)
        V.mark("gla o read", h)
        do(dve.scalar_tensor_tensor, out=g, in0=g, scalar=param(k, "glag", h, 1), in1=k.GS[:, h, :], op0=ALU.mult, op1=ALU.mult)
        V.mark("gla out", h)
        dve.wait_ge(*k.after("mix hi", 4 + h))
        low(k, dve, k.XL[:, 4 + h, 0:SEQ], g, k.XH[:, 4 + h, 0:SEQ], "mix lo", 4 + h)


def even_out_tensor(k, pe):
    rows_tensor(k, pe, "even rows", k.FIRST[("even_out",)], k.XH, k.XL)


def even_out_scalar(k, act):
    split_high(k, act, k.FIRST[("even_out",)] + 3)


def even_out_vector(k, dve):
    split_low(k, dve, k.FIRST[("even_out",)] + 3)
    for half in range(2):
        for t in range(XT):
            dve.wait_ge(*k.after("even rows", half, t))
            residual(k, dve, half, t, k.PS[:, 4 * half + t, :], 0, t)



QT = 4
QM = 8


def mlp_tensor(k, pe, s):
    c = k.FIRST[("mlp", s)]
    for f4 in range(QT):
        for m in range(QM):
            r = f4 * QM + m
            wh, wl = chunk_pair(k, pe, c + 8 * f4 + m // 2)
            if r >= 4:
                pe.wait_ge(*k.after("relu", s, r - 4))
            for f in range(DK):
                w = slice(((m % 2) * DK + f) * P, ((m % 2) * DK + f + 1) * P)
                mm = products(pe, k.PS[:, r % 4, :], wh[:, w], wl[:, w], k.XH[:, f, 0:SEQ], k.XL[:, f, 0:SEQ], f == 0, f == DK - 1)
            mm.then_inc(*k.T.step("mlp1", s, r))
            if m % 2:
                k.T.mark("used", k.SPLIT_NO[c + 8 * f4 + m // 2])
        for half in range(2):
            for q in range(2):
                n = c + 8 * f4 + 4 + 2 * half + q
                wh, wl = chunk_pair(k, pe, n)
                for t in range(XT):
                    if q == 0 and (f4 or half):
                        pe.wait_ge(*k.after("mlp y", s, 2 * f4 + half - 1, t))
                    for f in range(4):
                        if t == 0:
                            pe.wait_ge(*k.after("mlp lo", s, f4 * QM + 4 * q + f))
                        w = slice(f * HALF, f * HALF + HALF)
                        mm = products(pe, k.PS[:, 4 + t, :], k.HH[:, 4 * q + f, t * P:(t + 1) * P],
                                      k.HL[:, 4 * q + f, t * P:(t + 1) * P], wh[:, w], wl[:, w], q == 0 and f == 0, q == 1 and f == 3)
                    if q == 1 and t < XT - 1:
                        mm.then_inc(*k.T.step("mlp2", s, 2 * f4 + half, t))
                mm.then_inc(*k.T.step("used", k.SPLIT_NO[n]))
                if q:
                    k.T.mark("mlp2", s, 2 * f4 + half, XT - 1)


def mlp_scalar(k, act, s):
    c = k.FIRST[("mlp", s)]
    split_high(k, act, c + LOOK)
    for f4 in range(QT):
        for m in range(QM):
            r = f4 * QM + m
            act.wait_ge(*k.after("mlp1", s, r))
            if m % 2:
                split_high(k, act, c + 8 * f4 + m // 2 + LOOK + (m == QM - 1))
            if r >= 2:
                act.wait_ge(*k.after("mlp lo", s, r - 2))
            act.activation(k.MT[:, r % 2, :], k.PS[:, r % 4, :], ACT.Relu,
                           bias=param(k, "b1", 32 * (s // 2) + r, 1)).then_inc(*k.A.step("relu", s, r))
            act.wait_ge(*k.after("squared", s, r))
            if f4:
                act.wait_ge(*k.after("mlp2", s, 2 * f4 - 1, XT - 1))
            high(k, act, k.HH[:, m, :], k.MS[:, r % 2, :], "mlp hi", s, r)
        for n in range(4):
            if n:
                split_high(k, act, c + 8 * f4 + 4 + n + LOOK - (n == 3 and f4 == QT - 1 and 0))


def mlp_vector(k, dve, s):
    c = k.FIRST[("mlp", s)]
    split_low(k, dve, c + LOOK)
    dve.wait_ge(*k.after("row", f"b2{s}"))
    for f4 in range(QT):
        for m in range(QM):
            r = f4 * QM + m
            if m % 2:
                split_low(k, dve, c + 8 * f4 + m // 2 + LOOK + (m == QM - 1))
            dve.wait_ge(*k.after("relu", s, r))
            dve.wait_ge(*k.V.now())
            dve.tensor_tensor(k.MS[:, r % 2, :], k.MT[:, r % 2, :], k.MT[:, r % 2, :], ALU.mult).then_inc(*k.V.step("squared", s, r))
            dve.wait_ge(*k.after("mlp hi", s, r))
            low(k, dve, k.HL[:, m, :], k.MS[:, r % 2, :], k.HH[:, m, :], "mlp lo", s, r)
        for half in range(2):
            cols = slice(half * HALF, half * HALF + HALF)
            if half:
                split_low(k, dve, c + 8 * f4 + 6 + LOOK)
            for t in range(XT):
                if half == 0 and t == 0:
                    split_low(k, dve, c + 8 * f4 + 5 + LOOK)
                dve.wait_ge(*k.after("mlp2", s, 2 * f4 + half, t))
                y = k.YA[:, t, cols]
                dve.wait_ge(*k.V.now())
                dve.tensor_tensor(y, k.PS[:, 4 + t, :], y if f4 else row(k, f"b2{s}")[:, cols], ALU.add).then_inc(
                    *k.V.step("mlp y", s, 2 * f4 + half, t))
                if f4 == QT - 1:
                    residual(k, dve, half, t, y, s, t)
        split_low(k, dve, c + 8 * f4 + 7 + LOOK)
        if f4 == 0:
            k.V.mark("row done", f"b2{s}")



FT = 2 * DK
FH = 16


def fox_in_tensor(k, pe):
    c = k.FIRST[("fox_in",)]

    def sums(m):
        pe.wait_ge(*k.after("fox squares", m))
        if m >= 2:
            pe.wait_ge(*k.after("fox root", m - 2))
        pe.matmul(k.PS[:, 4 + m % 2, :], const(k, "pairs"), k.FX[:, m % 2, :], start=True, stop=True).then_inc(
            *k.T.step("fox sums", m))
    for m in range(FT):
        wh, wl = chunk_pair(k, pe, c + m // 2)
        if m >= 4:
            pe.wait_ge(*k.after("fox qk", m - 4))
        for f in range(DK):
            w = slice(((m % 2) * DK + f) * P, ((m % 2) * DK + f + 1) * P)
            mm = products(pe, k.PS[:, m % 4, :], wh[:, w], wl[:, w], k.XH[:, f, 0:SEQ], k.XL[:, f, 0:SEQ], f == 0, f == DK - 1)
        mm.then_inc(*k.T.step("fox", m))
        if m % 2:
            k.T.mark("used", k.SPLIT_NO[c + m // 2])
        if m:
            sums(m - 1)
    sums(FT - 1)
    wh, wl = chunk_pair(k, pe, c + 8)
    for f in range(DK):
        w = slice(f * 16, f * 16 + 16)
        mm = products(pe, k.PS[0:16, 6, :], wh[:, w], wl[:, w], k.XH[:, f, 0:SEQ], k.XL[:, f, 0:SEQ], f == 0, f == DK - 1)
    mm.then_inc(*k.T.step("used", k.SPLIT_NO[c + 8]))
    k.T.mark("fox f")
    for half in range(2):
        for q in range(2):
            wh, wl = chunk_pair(k, pe, c + 9 + 2 * half + q)
            for t in range(XT):
                if q == 0:
                    pe.wait_ge(*(k.after("fox v", 0, t) if half else k.after("fox qk", FT - 4 + t)))
                for f in range(4):
                    w = slice(f * HALF, f * HALF + HALF)
                    mm = products(pe, k.PS[:, t, :], k.XH[:, 4 * q + f, t * P:(t + 1) * P],
                                  k.XL[:, 4 * q + f, t * P:(t + 1) * P], wh[:, w], wl[:, w], q == 0 and f == 0, q == 1 and f == 3)
            mm.then_inc(*k.T.step("used", k.SPLIT_NO[c + 9 + 2 * half + q]))
        k.T.mark("fox v done", half)


def fox_in_scalar(k, act):
    c = k.FIRST[("fox_in",)]
    split_high(k, act, c + LOOK)
    for m in range(FT):
        act.wait_ge(*k.after("fox", m))
        if m % 2:
            split_high(k, act, c + m // 2 + LOOK)
        if m >= 2:
            act.wait_ge(*k.after("fox qk", m - 2))
        act.activation(k.FX[:, m % 2, :], k.PS[:, m % 4, :], ACT.Square).then_inc(*k.A.step("fox squares", m))
        act.wait_ge(*k.after("fox sums", m))
        act.activation(k.FX[:, m % 2, :], k.PS[:, 4 + m % 2, :], ACT.Sqrt, scale=1.0 / FOX_HD, bias=const(k, "eps")).then_inc(
            *k.A.step("fox root", m))
    split_high(k, act, c + 9)
    log_sigmoid_scalar(k, act, k.FL[:, 1, :], "fox")
    split_high(k, act, c + 10)
    for half in range(2):
        if half:
            split_high(k, act, c + 12)
        act.wait_ge(*k.after("fox v done", half))
        for t in range(XT):
            act.activation(k.FV[:, t, half * HALF:(half + 1) * HALF], k.PS[:, t, :], ACT.Copy).then_inc(*k.A.step("fox v", half, t))


def fox_in_vector(k, dve):
    V = k.V

    def do(f, *a, **b):
        dve.wait_ge(*V.now())
        f(*a, **b).then_inc(*V.step())
    c = k.FIRST[("fox_in",)]
    split_low(k, dve, c + LOOK)
    do(dve.tensor_scalar, k.GQ8[:, :], param(k, "foxq"), FOX_HD ** -0.5, None, ALU.mult)
    dve.wait_ge(*V.now())
    for m in range(FT):
        if m % 2:
            split_low(k, dve, c + m // 2 + LOOK)
        dve.wait_ge(*k.after("fox root", m))
        do(dve.reciprocal, k.FX[:, m % 2, :], k.FX[:, m % 2, :])
        dst = k.FQ[:, m, :] if m < DK else k.FK[:, m - DK, :]
        do(dve.scalar_tensor_tensor, out=dst, in0=k.PS[:, m % 4, :], scalar=k.GQ8[:, :] if m < DK else param(k, "foxk"),
           in1=k.FX[:, m % 2, :], op0=ALU.mult, op1=ALU.mult)
        V.mark("fox qk", m)
    split_low(k, dve, c + 9)
    dve.wait_ge(*k.after("fox f"))
    x, e, z, q = k.FL[:, 0, :], k.FL[:, 1, :], k.FX[0:16, 0, :], k.FX[0:16, 1, :]
    do(dve.tensor_scalar, x, k.PS[0:16, 6, :], param(k, "bf", rows=16), None, ALU.add)
    log_sigmoid_vector(k, dve, x, e, z, q, "fox")
    split_low(k, dve, c + 10)
    do(dve.memset, z, 1.0)
    do(dve.tensor_tensor_scan, e, z, x, 0.0, ALU.mult, ALU.add)
    do(dve.tensor_scalar, x, e, -1.0, None, ALU.mult)
    split_low(k, dve, c + 12)



FUNITS = FH * XT


def fox_tensor(k, pe):
    def scores(u):
        h, i = divmod(u, XT)
        m, r = h // 2, slice(64 * (h % 2), 64 * (h % 2) + 64)
        n = (i + 1) * P
        if u >= 2:
            pe.wait_ge(*k.after("fprob", u - 2))
        out = k.PS[:, u % 2, 0:n]
        pe.matmul(out, k.FQ[r, m, i * P:(i + 1) * P], k.FK[r, m, 0:n], start=True, stop=False)
        pe.matmul(out, const(k, "ident")[0:16, h:h + 1].to_broadcast([16, P]), k.FL[:, 0, 0:n], start=False, stop=False)
        pe.matmul(k.PS[:, u % 2, n - P:n], const(k, "ident"), const(k, "future"), start=False, stop=True).then_inc(
            *k.T.step("fscores", u))

    def turn(u):
        h, i = divmod(u, XT)
        pe.wait_ge(*k.after("fprob normed", u))
        if u >= 2:
            pe.wait_ge(*k.after("fpt", u - 2))
        for j in range(i + 1):
            mm = pe.transpose(k.PS[:, 2 + u % 2, j * P:(j + 1) * P], k.FP[:, u % 2, j * P:(j + 1) * P], const(k, "ident"))
        mm.then_inc(*k.T.step("fprob turned", u))

    def values(u):
        h, i = divmod(u, XT)
        pe.wait_ge(*k.after("fpt", u))
        if u >= 2:
            pe.wait_ge(*k.after("fo out", u - 2))
        out = k.PS[64 * (h % 2):64 * (h % 2) + 64, 4 + u % 2, 0:P]
        for j in range(i + 1):
            mm = pe.matmul(out, k.FV[:, j, h * 64:(h + 1) * 64], k.FPT[u % 2][:, j * P:(j + 1) * P], start=(j == 0), stop=(j == i))
        mm.then_inc(*k.T.step("fo", u))
    scores(0)
    scores(1)
    for u in range(FUNITS):
        turn(u)
        if u + 2 < FUNITS:
            scores(u + 2)
        if u >= 1:
            values(u - 1)
    values(FUNITS - 1)


def fox_scalar(k, act):
    def prob(u):
        n = (u % XT + 1) * P
        act.wait_ge(*k.after("ftop", u))
        if u >= 2:
            act.wait_ge(*k.after("fprob turned", u - 2))
        act.activation(k.FP[:, u % 2, 0:n], k.PS[:, u % 2, 0:n], ACT.Exp, bias=k.TOP[:, 2 + u % 2:3 + u % 2],
                       accum_out=k.SUM[:, u % 2:u % 2 + 1]).then_inc(*k.A.step("fprob", u))
    prob(0)
    for u in range(FUNITS):
        n = (u % XT + 1) * P
        if u + 1 < FUNITS:
            prob(u + 1)
        act.wait_ge(*k.after("fprob turned", u))
        if u >= 2:
            act.wait_ge(*k.after("fo", u - 2))
        act.activation(k.FPT[u % 2][:, 0:n], k.PS[:, 2 + u % 2, 0:n], ACT.Copy).then_inc(*k.A.step("fpt", u))


def fox_vector(k, dve):
    V = k.V

    def top(u):
        n = (u % XT + 1) * P
        dve.wait_ge(*k.after("fscores", u))
        if u >= 2:
            dve.wait_ge(*k.after("fprob", u - 2))
        dve.wait_ge(*V.now())
        dve.tensor_reduce(k.TOP[:, u % 2:u % 2 + 1], k.PS[:, u % 2, 0:n], AX.X, ALU.max).then_inc(*V.step())
        dve.wait_ge(*V.now())
        dve.tensor_scalar(k.TOP[:, 2 + u % 2:3 + u % 2], k.TOP[:, u % 2:u % 2 + 1], -1.0, None, ALU.mult).then_inc(
            *V.step("ftop", u))
    def normed(u):
        n = (u % XT + 1) * P
        dve.wait_ge(*k.after("fprob", u))
        dve.wait_ge(*V.now())
        dve.reciprocal(k.TOP[:, 4 + u % 2:5 + u % 2], k.SUM[:, u % 2:u % 2 + 1]).then_inc(*V.step())
        dve.wait_ge(*V.now())
        dve.tensor_scalar(k.FP[:, u % 2, 0:n], k.FP[:, u % 2, 0:n], k.TOP[:, 4 + u % 2:5 + u % 2], None, ALU.mult).then_inc(
            *V.step("fprob normed", u))

    def out(u):
        h, i = divmod(u, XT)
        r = slice(64 * (h % 2), 64 * (h % 2) + 64)
        dve.wait_ge(*k.after("fo", u))
        dve.tensor_copy(k.FQ[r, h // 2, i * P:(i + 1) * P], k.PS[r, 4 + u % 2, 0:P]).then_inc(*V.step("fo out", u))
    top(0)
    normed(0)
    top(1)
    for u in range(FUNITS):
        if u + 1 < FUNITS:
            normed(u + 1)
        if u + 2 < FUNITS:
            top(u + 2)
        if u >= 1:
            out(u - 1)
    out(FUNITS - 1)



def fox_out_tensor(k, pe):
    c = k.FIRST[("fox_out",)]
    for m in range(DK):
        wh, wl = chunk_pair(k, pe, c + m // 2)
        if m >= 4:
            pe.wait_ge(*k.after("gate sigmoid", m - 4))
        for f in range(DK):
            w = slice(((m % 2) * DK + f) * P, ((m % 2) * DK + f + 1) * P)
            mm = products(pe, k.PS[:, m % 4, :], wh[:, w], wl[:, w], k.XH[:, f, 0:SEQ], k.XL[:, f, 0:SEQ], f == 0, f == DK - 1)
        mm.then_inc(*k.T.step("fox g", m))
        if m % 2:
            k.T.mark("used", k.SPLIT_NO[c + m // 2])
    pe.wait_ge(*k.after("gated lo", DK - 1))
    rows_tensor(k, pe, "fox rows", c + 4, k.OH, k.OL)


def fox_out_scalar(k, act):
    c = k.FIRST[("fox_out",)]
    split_high(k, act, c + LOOK)
    for m in range(DK):
        act.wait_ge(*k.after("fox g", m))
        if m % 2:
            split_high(k, act, c + m // 2 + LOOK)
        if m >= 2:
            act.wait_ge(*k.after("gated lo", m - 2))
        act.activation(k.FX[:, m % 2, :], k.PS[:, m % 4, :], ACT.Sigmoid).then_inc(*k.A.step("gate sigmoid", m))
        act.wait_ge(*k.after("gated", m))
        high(k, act, k.OH[:, m, :], k.FX[:, m % 2, :], "gated hi", m)
    split_high(k, act, c + 7)


def fox_out_vector(k, dve):
    c = k.FIRST[("fox_out",)]
    split_low(k, dve, c + LOOK)
    for m in range(DK):
        if m % 2:
            split_low(k, dve, c + m // 2 + LOOK)
        dve.wait_ge(*k.after("gate sigmoid", m))
        dve.tensor_tensor(k.FX[:, m % 2, :], k.FX[:, m % 2, :], k.FQ[:, m, :], ALU.mult).then_inc(*k.V.step("gated", m))
        dve.wait_ge(*k.after("gated hi", m))
        low(k, dve, k.OL[:, m, :], k.FX[:, m % 2, :], k.OH[:, m, :], "gated lo", m)
    split_low(k, dve, c + 7)
    for half in range(2):
        for t in range(XT):
            dve.wait_ge(*k.after("fox rows", half, t))
            residual(k, dve, half, t, k.PS[:, 4 * half + t, :], 2, t)


def place_rest(k, nc, top):
    k.QN = k.at("q_nope", [P, HEADS, SEQ], k.SCR)
    k.KT = k.at("k_nope", [P, HEADS, KEYS], k.end)
    k.VAL = k.at("values", [P, XT, D], k.end)
    k.KR = k.at("k_rope", [P, KEYS], k.end)
    k.CB = k.at("c_rows", [P, XT + 1, CWID], k.SCR)
    k.CN = k.at("c_norm", [P, XT + 1, KVR], k.end)
    k.KRD = k.at("k_rope_rows", [P, XT + 1, P], k.end)
    k.TRA = k.at("rotate_a", [P, XT + 1, ROPE // 2], k.end)
    k.TRB = k.at("rotate_b", [P, XT + 1, ROPE // 2], k.end)
    k.CKH = k.at("ck_high", [P, 2, KEYS], k.XHAT, F32R)
    k.CKL = k.at("ck_low", [P, 2, KEYS], k.end, F32R)
    k.CQN = k.at("cq_norm", [P, XT, QR], k.SCR)
    k.QRT = k.at("q_rope", [P, HEADS // 2, SEQ], k.XHAT)
    a = k.end
    k.QRB = k.at("q_rope_rows", [P, 2, SEQ], a)
    k.TQA = k.at("rotate_c", [P, HEADS, ROPE // 2], k.end)
    k.TQB = k.at("rotate_d", [P, HEADS, ROPE // 2], k.end)
    k.PR = [k.at("prob_even", [P, KEYS - P], a), k.at("prob_odd", [P, KEYS], k.end)]
    k.PT = [k.at("prob_turned_even", [P, XT, P], k.end), k.at("prob_turned_odd", [P, XT + 1, P], k.end)]
    k.CQH = k.at("cq_high", [P, 3, SEQ], k.XLAT, F32R)
    k.CQL = k.at("cq_low", [P, 3, SEQ], k.end, F32R)
    k.OTH = k.at("o_high", [P, HEADS, SEQ], k.SCR, F32R)
    k.OTL = k.at("o_low", [P, HEADS, SEQ], k.XLAT, F32R)
    k.ACC = k.at("ada_sums", [P, 3 * D], k.SCR)
    k.UT = k.at("u_tile", [P, 2, SEQ], k.end)
    k.XR = k.at("rg_in", [P, RGT, SEQ + 3], k.SCR)
    k.YR = k.at("rg_gate", [P, RGT, SEQ], k.end)
    yr = k.end - RGT * SEQ * 4
    k.GQ = k.at("gla_q", [P, 2, SEQ], k.end)
    k.GK = k.at("gla_k", [P, 2, SEQ], k.end)
    k.GS = k.at("gla_g", [P, GH, SEQ], k.end)
    k.GV = k.at("gla_v", [P, XT, SEQ], k.end)
    k.ZL = k.at("gla_z", [16, SEQ], k.end)
    k.LT = k.at("even_tmp", [P, 5, SEQ], k.end)
    lt = k.end - 5 * SEQ * 4
    k.WUP = k.at("gla_w_up", [16, 2 * P], k.keep)
    k.RESET = k.at("chunk_reset", [P, SEQ], k.SCR)
    k.AT = k.at("gla_scores", [P, 2, SEQ], k.end)
    k.KD = k.at("gla_k_decayed", [P, 2, SEQ], yr)
    k.KET = k.at("gla_k_end", [P, 2, XT, P], k.end)
    k.ST = k.at("gla_states", [P, 2, NCH, P], lt)
    k.GT = k.at("gla_tmp", [P, 2, SEQ], yr + 2 * SEQ * 4)
    k.RESID = k.at("residual_tmp", [P, 2, HALF], k.SCR)
    k.FL = k.at("fox_forget", [16, 2, SEQ], k.SPARE)
    k.HH = k.at("mlp_high", [P, QM, SEQ], k.SCR + 2 * HALF * 4, F32R)
    k.HL = k.at("mlp_low", [P, QM, SEQ], k.end, F32R)
    k.YA = k.at("mlp_y", [P, XT, D], k.end)
    k.MT = k.at("mlp_relu", [P, 2, SEQ], k.SPARE)
    k.MS = k.at("mlp_square", [P, 2, SEQ], k.SCR)
    k.FQ = k.at("fox_q", [P, DK, SEQ], k.SCR)
    fk = k.end
    k.FK = k.at("fox_k", [P, DK, SEQ], fk)
    fv = k.end
    k.FV = k.at("fox_v", [P, XT, D], fv)
    fx = k.end
    k.FX = k.at("fox_tmp", [P, 2, SEQ], fx)
    k.FP = k.at("fox_prob", [P, 2, SEQ], fx)
    k.FPT = [k.at("fox_prob_turned_even", [P, SEQ - P], k.end), k.at("fox_prob_turned_odd", [P, SEQ], k.SPARE + SEQ * 4)]
    k.OH = k.at("fox_high", [P, DK, SEQ], fk, F32R)
    k.OL = k.at("fox_low", [P, DK, SEQ], fv, F32R)



SCALAR = {"pool": pool_scalar, "route": route_scalar, "moe": moe_scalar, "latent": latent_scalar, "query":
          query_scalar, "attend": attend_scalar, "attout": attout_scalar, "last": last_scalar, "ada": ada_scalar,
          "layernorm": layernorm_scalar, "even_in": even_in_scalar, "lru": lru_scalar, "gla": gla_scalar,
          "even_out": even_out_scalar, "mlp": mlp_scalar, "fox_in": fox_in_scalar, "fox": fox_scalar, "fox_out":
          fox_out_scalar}
VECTOR = {"pool": pool_vector, "route": route_vector, "moe": moe_vector, "combine": combine_vector, "latent":
          latent_vector, "query": query_vector, "attend": attend_vector, "attout": attout_vector, "last":
          last_vector, "ada": ada_vector, "layernorm": layernorm_vector, "even_in": even_in_vector, "lru":
          lru_vector, "gla": gla_vector, "even_out": even_out_vector, "mlp": mlp_vector, "fox_in": fox_in_vector,
          "fox": fox_vector, "fox_out": fox_out_vector}
TENSOR = {"pool": pool_tensor, "route": route_tensor, "moe": moe_tensor, "latent": latent_tensor, "query":
          query_tensor, "attend": attend_tensor, "attout": attout_tensor, "ada": ada_tensor, "even_in":
          even_in_tensor, "lru": lru_tensor, "gla": gla_tensor, "even_out": even_out_tensor, "mlp": mlp_tensor,
          "fox_in": fox_in_tensor, "fox": fox_tensor, "fox_out": fox_out_tensor}
GPSIMD = {"pool": pool_gpsimd, "route": route_gpsimd, "moe": moe_gpsimd, "combine": combine_gpsimd, "lru":
          lru_gpsimd}


def stage_list():
    return ([("pool",), ("route", 0, XT + 1), ("moe", 0), ("combine", 0, XT + 1), ("latent",), ("query",), ("attend",), ("attout",),
             ("route", 1, XT), ("moe", 1), ("combine", 1, XT), ("last",)]
            + [("ada", 0), ("even_in",), ("lru",), ("gla",), ("even_out",), ("layernorm", 0)]
            + [("ada", 1), ("mlp", 1), ("layernorm", 1)]
            + [("ada", 2), ("fox_in",), ("fox",), ("fox_out",), ("layernorm", 2)]
            + [("ada", 3), ("mlp", 3), ("layernorm", 3)])


def chunk_list(dram, stages):
    out, moe0, unused = [], [], []
    names = {"pool": ["a_w"], "latent": ["kv"], "query": ["q"], "attout": ["wo"], "even_in": ["evin", "evz"],
             "even_out": ["evout"], "fox_in": ["foxqk", "foxf", "foxv"], "fox_out": ["foxg", "foxout"]}
    first = {}
    for st in stages:
        first[st] = len(out)
        if st[0] == "moe":
            moe0.append(len(out))
            out += [(None, CW, True)] * (3 * NBLK)
            follows = [x for x in stages[stages.index(st) + 1:] if x[0] in names]
            if st[1] == 1 or not follows:
                unused.append(len(out))
                out += [(dram["filler"][0], CW, True)] * MOE_LOOK
            continue
        if st[0] in ("ada", "mlp"):
            parts, split = [dram[st[0]][st[1] if st[0] == "ada" else st[1] // 2]], st[0] == "mlp"
        else:
            parts, split = [dram[n] for n in names.get(st[0], [])], True
        out += [(src[c], src.shape[2], split) for src in parts for c in range(src.shape[0])]
    return out, moe0, unused, first


def program(nc, ctx, marks, dram, out, stop=None):
    k = Kernel(nc, ctx, marks, dram, stop)
    stages = stage_list()
    if stop:
        stages = stages[:stop]
    chunks, k.MOE0, k.UNUSED, first = chunk_list(dram, stages)
    k.FIRST = first
    k.CH = [(c[0], c[1]) for c in chunks]
    k.SPLIT = [c[2] for c in chunks]
    k.SPLIT_NO, n = [], 0
    for s in k.SPLIT:
        k.SPLIT_NO.append(n)
        n += s
    k.high_next = k.low_next = 0

    k.xn_d = nc.dram_tensor("xn_rows", ((XT + 1) * P, D), F32, kind="Internal").ap()
    k.y_d = nc.dram_tensor("expert_rows", (2 * (XT + 1) * P, D), F32, kind="Internal").ap()
    k.tab_d = nc.dram_tensor("block_table", (P * TABW, 2), I32, kind="Internal").ap()
    k.fc_d = nc.dram_tensor("spare", (P, P), F32, kind="Internal").ap()

    k.end = 16512
    k.RAW = [k.at(f"raw{i}", [P, CW], k.end) for i in range(RAW_SLOTS)]
    k.WH = [k.at(f"w_high{i}", [P, CW], k.end, F32R) for i in range(SPLIT_SLOTS)]
    k.WL = [k.at(f"w_low{i}", [P, CW], k.end, F32R) for i in range(SPLIT_SLOTS)]
    k.H = k.at("h", [P, XT + 1, D], k.end)
    k.SPARE = k.end - D * 4
    k.CONST = k.at("const", [P, CONSTW], k.end)
    k.PARAM = k.at("param", [P, PARAMW], k.end)
    k.ROWB = k.at("rows", [P, ROW_SLOTS, D], k.end)
    k.SS = k.at("ss", [P, 8], k.end)
    k.RT = k.at("rt", [P, 8], k.end)
    k.RS = k.at("rs", [P, 8], k.end)
    k.TOP = k.at("tops", [P, 8], k.end)
    k.SUM = k.at("sums", [P, 8], k.end)
    k.CS = k.at("condition", [P, DK], k.end)
    k.SHC = k.at("shift", [P, DK], k.end)
    k.SCC = k.at("scale", [P, DK], k.end)
    k.GQ8 = k.at("fox_q_gain", [P, 1], k.end)
    k.DCY = k.at("gla_decay", [P, 2, NCH], k.end)
    k.PRIME = k.at("prime", [P, 3, 8], k.end)
    k.LM = k.at("lambda", [P, 5, RGT], k.end)
    k.BN = k.at("bn", [P, XT, 12], k.end)
    k.MV = k.at("mean_var", [P, XT, 2], k.end)
    k.XHAT = k.end
    k.XH = k.at("x_high", [P, DK, KEYS], k.end, F32R)
    k.XLAT = k.end
    k.XL = k.at("x_low", [P, DK, KEYS], k.end, F32R)
    k.SCR = k.end
    k.WHX = k.at("w_high_extra", [P, CW], k.XHAT, F32R)
    k.WLX = k.at("w_low_extra", [P, CW], k.end, F32R)
    k.XGH = [k.at(f"xg_high{i}", [P, DK, P], k.end, F32R) for i in range(2)]
    k.XGL = [k.at(f"xg_low{i}", [P, DK, P], k.end, F32R) for i in range(2)]
    k.end = k.SCR
    k.PS = ctx.enter_context(nc.psum_tensor("psum", [P, 8, HALF], F32))
    top = nc.sbuf_usable_end // 32 * 32
    k.XN = k.at("xn", [P, 2, D], k.SCR)
    k.SQ = k.at("squares", [P, D], k.end)
    a = k.SQ_END = k.end
    k.XP = k.at("xp", [P, DK, META + KEYS], a)
    k.PA = k.at("window_a", [P, 2, META + KEYS], k.end)
    k.PB = k.at("window_b", [P, 2, META + KEYS], k.end)
    k.PL = k.at("pooled", [P, 2, KEYS], k.end)
    k.TMPAT = k.end
    k.TMP = k.at("mix_tmp", [P, 1, HALF], k.SCR)
    k.RC = k.at("rcnt", [P, 4, KEYS], k.TMPAT)
    k.XF = k.at("xf", [P, 2, DK, P], a)
    k.WR = k.at("router_w", [P, DK, NG + NE], k.end)
    k.LG = k.at("route_lg", [P, XT + 1, NG + NE], k.end)
    k.LE = k.at("route_le", [P, XT + 1, NE], k.end)
    k.HIT1 = k.at("route_hit1", [P, XT + 1, NE], k.end)
    k.HIT2 = k.at("route_hit2", [P, XT + 1, NE], k.end)
    k.PICK = k.at("route_pick", [P, XT + 1, NE], k.end)
    k.POS = k.at("route_pos", [P, XT + 1, NE], k.end)
    k.DG = k.at("route_dg", [P, XT + 1, NG], k.end)
    k.EG = k.at("route_eg", [P, XT + 1, NG], k.end)
    k.G1H = k.at("route_g1h", [P, XT + 1, NG], k.end)
    k.PEN = k.at("route_pen", [P, XT + 1, NG], k.end)
    k.RM = k.at("route_rm", [P, 8, XT + 1], k.end)
    k.GAP = k.at("route_gap", [P, XT + 1], k.end)
    k.E2 = k.at("route_e2", [P, XT + 1], k.end)
    k.CNT = k.at("route_cnt", [P, 3, NE], k.end)
    k.CMP = k.at("route_cmp", [P, TABW, NE], k.end)
    k.BE = k.at("route_be", [P, TABW], k.end)
    k.keep = top - 1152
    k.GATE = k.at("gate", [P, 2, XT + 1], k.keep)
    k.DEST = k.at("dest", [P, 2, XT + 1], k.end, I32)
    k.AID = k.at("assignments", [P, 4 * (XT + 1)], k.end, I32)
    k.TABI = k.at("table_blank", [P, 2 * TABW], k.end, I32)
    k.TAB = k.at("table", [P, 2 * TABW], k.end, I32)
    k.IDX = k.at("index_columns", [P, 4], k.end, I32)
    k.BEI = k.at("block_chunk", [P, TABW], k.end, I32)
    k.XG = k.at("xg", [P, 2, D], k.SCR)
    k.YB = k.at("yb", [P, 2, D], k.end)
    k.SILU = k.at("silu", [P, DE], k.end)
    k.HID = k.at("hidden", [P, DE], k.end)
    k.HTH = k.at("hidden_high", [P, 2, P], k.end, F32R)
    k.HTL = k.at("hidden_low", [P, 2, P], k.end, F32R)
    k.YC = k.at("yc", [P, 2, 2 * D], k.SCR)
    place_rest(k, nc, top)

    def run(kind, parts, eng, prog):
        for n, st in enumerate(stages):
            f = parts.get(st[0])
            if f is None:
                prog.mark("end", n, kind)
                continue
            if n:
                for other in ("scalar", "vector", "tensor", "gpsimd"):
                    if other != kind:
                        eng.wait_ge(*k.after("end", n - 1, other))
                eng.wait_ge(*prog.now())
            f(k, eng, *st[1:], *((first[st],) if st[0] == "moe" else ()))
            prog.mark("end", n, kind)

    block = ctx.enter_context(nc.Block())

    @block.sync
    def _(sync):
        sync.dma_start(k.CONST[:, :], dram["const"]).then_inc(*k.counter("const_loaded").step("const", by=16))
        sync.dma_start(k.H[:, 0:XT, :], dram["x"].rearrange("(t p) d -> p t d", p=P)).then_inc(
            *k.counter("x_loaded").step("x", by=16))
        sync.wait_ge(*k.after("meta zero"))
        sync.dma_start(k.H[0:META, XT, :], dram["meta"]).then_inc(*k.counter("meta_loaded").step("meta", by=16))
        sync.dma_start(k.PARAM[:, :], dram["param"]).then_inc(*k.counter("param_loaded").step("param", by=16))
        sync.dma_start(k.AID[:, :], dram["aid"]).then_inc(*k.counter("aid_loaded").step("aid", by=16))
        sync.dma_start(k.TABI[:, :], dram["tabi"]).then_inc(*k.counter("tabi_loaded").step("tabi", by=16))
        c = 0
        while c < len(k.CH):
            if c in k.MOE0:
                moe_sync(k, sync, k.MOE0.index(c), c)
                c += 3 * NBLK
            else:
                load_chunk(k, sync, c)
                c += 1
        sync.wait_ge(*k.after("end", len(stages) - 1, "vector"))
        sync.wait_ge(*k.after("end", len(stages) - 1, "scalar"))
        sync.dma_start(out.rearrange("(t p) d -> p t d", p=P), k.H[:, 0:XT, :]).then_inc(
            *k.counter("out_stored").step("out", by=16))
        sync.wait_ge(*k.after("out"))

    @block.gpsimd
    def _(pool):
        pool.memset(k.H[:, XT, :], 0.0).then_inc(*k.G.step("meta zero"))
        k.row_next = 0

        def rows(upto):
            while k.row_next <= upto and k.row_next < len(ROWS):
                r = k.row_next
                k.row_next += 1
                if ("row done", ROWS[r]) not in marks and marks.get("complete"):
                    break
                if r >= ROW_SLOTS:
                    pool.wait_ge(*k.after("row done", ROWS[r - ROW_SLOTS]))
                pool.dma_start(k.ROWB[:, r % ROW_SLOTS, :], dram["rows"][r]).then_inc(
                    *k.counter(f"row{r % ROW_SLOTS}_loaded").step("row", ROWS[r], by=16))
        k.rows = rows
        rows(1)
        for n, st in enumerate(stages):
            f = GPSIMD.get(st[0])
            if f:
                if n:
                    for other in ("scalar", "vector", "tensor"):
                        pool.wait_ge(*k.after("end", n - 1, other))
                if st[0] == "route":
                    pool.wait_ge(*k.after("aid"))
                    pool.wait_ge(*k.after("tabi"))
                f(k, pool, *st[1:], *((first[st],) if st[0] == "moe" else ()))
            k.G.mark("end", n, "gpsimd")
            if st[0] == "pool":
                rows(3)
            elif st[0] == "combine":
                rows(5 if st[1] == 0 else ROWS.index("lnb0"))
            elif st[0] == "layernorm" and st[1] < 3:
                rows(ROWS.index(f"lnb{st[1] + 1}"))

    @block.scalar
    def _(act):
        act.wait_ge(*k.after("const"))
        act.wait_ge(*k.after("param"))
        act.wait_ge(*k.after("x"))
        act.wait_ge(*k.after("meta"))
        run("scalar", SCALAR, act, k.A)

    @block.vector
    def _(dve):
        dve.wait_ge(*k.after("const"))
        dve.wait_ge(*k.after("param"))
        dve.wait_ge(*k.after("x"))
        dve.wait_ge(*k.after("meta"))
        run("vector", VECTOR, dve, k.V)

    @block.tensor
    def _(pe):
        pe.wait_ge(*k.after("const"))
        run("tensor", TENSOR, pe, k.T)
    marks["complete"] = True



def _constants(np):
    c = np.zeros((P, CONSTW), np.float32)
    def put(name, a):
        at, w = _C[name]
        c[:, at:at + w] = a
    i = np.arange(P)
    put("ident", np.eye(P))
    put("ones", 1.0)
    put("upper", i[:, None] < i[None, :])
    put("future", np.where(i[None, :] <= i[:, None], 0.0, -BIG))
    put("chunkmask", (i[:, None] // 64 == i[None, :] // 64) & (i[:, None] <= i[None, :]))
    put("pairs", i[:, None] // 64 == i[None, :] // 64)
    put("rev", np.concatenate([NG - np.arange(NG), NE - np.arange(NE)])[None, :])
    tok = np.arange(XT + 1)[None, :] * P + i[:, None]
    put("valid", tok < KEYS)
    put("absent", np.where(tok < KEYS, 0.0, 100000.0))
    put("eps", RMS_EPS)
    put("lneps", LN_EPS)
    put("one", 1.0)
    put("blocks", np.arange(TABW)[None, :])
    pos = np.where(tok < SEQ, tok + META, tok - SEQ).astype(np.float32)
    freq = (np.float32(10000.0) ** (-np.arange(0, ROPE, 2, dtype=np.float32) / np.float32(ROPE))).astype(np.float32)
    ang = (pos[:, :, None] * freq[None, None, :]).astype(np.float32)
    put("cos", np.cos(ang).reshape(P, -1))
    put("sin", np.sin(ang).reshape(P, -1))
    t = np.arange(KEYS)
    rcnt = np.stack([1.0 / np.minimum(t + 1, w) for w in (2, 4, 8, 16)]).astype(np.float32)
    aid = np.stack([np.stack([tok, 2 * tok + n], -1) for n in range(2)], 2).reshape(P, -1).astype(np.int32)
    tabi = np.tile(np.array([0, 1 << 20], np.int32), (P, TABW))
    return {"const": c, "rcnt": np.broadcast_to(rcnt, (P, 4, KEYS)), "aid": aid, "tabi": tabi}


def _params(np, f):
    r = np.zeros((P, PARAMW), np.float32)
    def put(name, a):
        at, w = _R[name]
        r[:, at:at + w] = a
    def cols(v):
        return v.reshape(-1, P).T
    put("adab", np.concatenate([cols(f["ada_b_2"].reshape(4, -1)[s, :2 * D]) for s in range(4)], 1))
    put("c", cols(f["c_2"].reshape(-1)))
    put("convw", np.concatenate([cols(f["ev_conv_w_2"][0, j]) for j in range(4)], 1))
    put("convb", cols(f["ev_conv_b_2"][0]))
    put("ba", cols(f["ev_rg_ba_2"][0]))
    put("bx", cols(f["ev_rg_bx_2"][0]))
    put("lam", cols(f["ev_rg_lam_2"][0]))
    put("bup", cols(f["ev_gla_b_up_2"][0]))
    put("glag", cols(f["ev_gla_norm_g_2"][0]))
    put("foxq", np.concatenate([f["od_q_norm_g_2"][0]] * 2)[:, None])
    put("foxk", np.concatenate([f["od_k_norm_g_2"][0]] * 2)[:, None])
    bf = np.zeros((P, 1), np.float32)
    bf[:16, 0] = f["od_b_f_2"][0]
    put("bf", bf)
    put("b1", np.concatenate([cols(f["mlp_b1_2"][s]) for s in range(2)], 1))
    put("qrow", f["b_q_norm"][0][None])
    put("kvrow", f["kv_lat_norm"][None])
    put("rbias", np.concatenate([f["router_g_bias"][0], f["router_e_bias"][0], f["router_g_bias"][1], f["router_e_bias"][1]])[None])
    rows = {"a_norm": f["a_norm"][0], "a_scale": f["a_scale"][0], "ffn0": f["ffn_norm"][0], "kv_norm": f["kv_norm"],
            "b_norm": f["b_norm"][0], "ffn1": f["ffn_norm"][1], "final": f["final_norm"]}
    for s in range(4):
        rows[f"gate{s}"] = f["ada_b_2"][s // 2, s % 2, 2 * D:]
        rows[f"b2{s}"] = f["mlp_b2_2"][s // 2]
        rows[f"lng{s}"] = f["ln_g_2"][s // 2, s % 2]
        rows[f"lnb{s}"] = f["ln_b_2"][s // 2, s % 2]
    return {"param": r, "rows": np.broadcast_to(np.stack([rows[n] for n in ROWS])[:, None, :], (len(ROWS), P, D))}


def _pack(np, w):
    return w.reshape(-1, P, w.shape[1]).transpose(1, 0, 2)


def _tiles(np, w):
    k, n = w.shape
    return w.reshape(k // P, P, n // P, P).transpose(2, 1, 0, 3).reshape(n // P, P, k)


def _group(np, a, n):
    m, p, w = a.shape
    return a.reshape(m // n, n, p, w).transpose(0, 2, 1, 3).reshape(m // n, p, n * w)


def _halves(np, w):
    k, n = w.shape
    a = w.reshape(k // (4 * P), 4, P, n // HALF, HALF).transpose(3, 0, 2, 1, 4)
    return a.reshape(-1, P, 4 * HALF)


def _weights(np, f):
    out = {}
    out["a_w"] = f["a_w"][0].reshape(4, 2, P, POOL_G).transpose(2, 0, 1, 3).reshape(1, P, CW)
    wr = [np.concatenate([f["router_g"][L], f["router_e"][L]], 1) for L in range(2)]
    out["wr"] = np.stack([_pack(np, w) for w in wr])
    gu = np.concatenate([f["w_gate"], f["w_up"]], 3).reshape(2, NE, 2, 4, P, 2 * DE).transpose(0, 1, 2, 4, 3, 5).reshape(2, NE, 2, P, CW)
    dn = f["w_down"].reshape(2, NE, 1, 2, P, D).transpose(0, 1, 2, 4, 3, 5).reshape(2, NE, 1, P, CW)
    out["moe"] = np.concatenate([gu, dn], 2).reshape(2 * NE * 3, P, CW)
    out["filler"] = out["a_w"]

    def wide(a):
        return np.concatenate([a, np.zeros(a.shape[:2] + (CW - a.shape[2],), a.dtype)], 2)
    dkv = f["w_dkv"].reshape(2, 4, P, CWID).transpose(0, 2, 1, 3).reshape(2, P, 4 * CWID)
    uk = _group(np, _tiles(np, f["w_uk"].reshape(KVR, HEADS * NOPE)), HEADS)
    uv = _pack(np, f["w_uv"].reshape(KVR, HEADS * VD)).reshape(1, P, CW)
    out["kv"] = np.concatenate([wide(dkv), uk, uv])
    dq = f["b_w_dq"][0].reshape(2, 4, P, QR).transpose(0, 2, 1, 3).reshape(2, P, 4 * QR)
    uq = f["b_w_uq"][0]
    rope = _pack(np, uq[:, :, NOPE:].reshape(QR, HEADS * ROPE)).reshape(1, P, 4 * QR)
    nope = _group(np, _tiles(np, uq[:, :, :NOPE].reshape(QR, HEADS * NOPE)), 4)
    out["q"] = np.concatenate([dq, rope, nope])
    out["wo"] = _halves(np, f["b_w_o"][0])
    ev = f["ev_w_in_2"][0]
    out["evin"] = np.concatenate([_group(np, _tiles(np, np.concatenate([ev[:, :1536], ev[:, 2048:2560]], 1)), 2),
                                  _halves(np, ev[:, 1536:2048])])
    out["evz"] = _pack(np, ev[:, 2560:]).reshape(1, P, -1)
    out["evout"] = _halves(np, f["ev_w_out_2"][0])
    od = f["od_w_in_2"][0]
    out["foxqk"] = _group(np, _tiles(np, od[:, :2 * D]), 2)
    out["foxf"] = _pack(np, od[:, 4 * D:]).reshape(1, P, -1)
    out["foxv"] = _halves(np, od[:, 2 * D:3 * D])
    out["foxg"] = _group(np, _tiles(np, od[:, 3 * D:4 * D]), 2)
    out["foxout"] = _halves(np, f["od_w_out_2"][0])
    out["ada"] = f["ada_w_2"].reshape(4, DK, P, 2, ADAW).transpose(0, 1, 3, 2, 4).reshape(4, 2 * DK, P, ADAW)
    mlp = []
    for L in range(2):
        w1, w2 = f["mlp_w1_2"][L], f["mlp_w2_2"][L]
        for q in range(QT):
            s = slice(q * D, (q + 1) * D)
            mlp += [_group(np, _tiles(np, w1[:, s]), 2), _halves(np, w2[s])]
    out["mlp"] = np.concatenate(mlp).reshape(2, -1, P, CW)
    rg = np.zeros((P, 2, RGT, P), np.float32)
    for g, w in enumerate((f["ev_rg_wa_2"][0], f["ev_rg_wx_2"][0])):
        for b in range(8):
            r = slice(64 * (b % 2), 64 * (b % 2) + 64)
            rg[r, g, b // 2, r] = w[b]
    out["rg"] = rg.reshape(P, D)
    out["wup"] = f["ev_gla_w_up_2"][0]
    return out


_SHAPE = (1, SEQ, D)
_STOP = None


def kernel(**inputs):
    import numpy as _np
    import concourse.bacc as _bacc
    from concourse.bass_utils import run_bass_kernel_spmd as _run

    f = {n: _np.asarray(a) for n, a in inputs.items()}
    arrays = {"x": f["x"].reshape(SEQ, D), "meta": f["meta_tokens"]}
    arrays.update(_constants(_np))
    arrays.update(_params(_np, f))
    arrays.update(_weights(_np, f))
    arrays = {f"in_{n}": _np.ascontiguousarray(a) for n, a in arrays.items()}
    marks = {}
    for _ in range(2):
        nc = _bacc.Bacc("TRN2", target_bir_lowering=False, num_devices=1)
        dram = {n[3:]: nc.dram_tensor(n, a.shape, mybir.dt.from_np(a.dtype), kind="ExternalInput").ap()
                for n, a in arrays.items()}
        out = nc.dram_tensor("out", (SEQ, D), F32, kind="ExternalOutput").ap()
        with ExitStack() as ctx:
            program(nc, ctx, marks, dram, out, _STOP)
    r = _run(nc, [arrays], core_ids=[0])
    return r.results[0]["out"].reshape(_SHAPE)
```
